# Optimizing a Trainium2 kernel written in Bass

```python
import jax, jax.numpy as jnp
from jax import lax
import numpy as np

D_MODEL = 1024
BATCH = 1
SEQ = 1024
DEPTH = 1

GRID_W = 64
HEAD_DIM = 64
NA_HEADS = 8
NA_KH_MAX = 8
NA_KW = 16
SWA_HEADS = 8
SWA_KV_HEADS = 2
SWA_WINDOW = 128
SWA_BLOCK = 128
ROPE_THETA = 10000.0
NA_WIDTH = NA_HEADS * HEAD_DIM
SWA_WIDTH = SWA_HEADS * HEAD_DIM
SWA_KV_WIDTH = SWA_KV_HEADS * HEAD_DIM
MIX_WIDTH = NA_WIDTH + SWA_WIDTH
QKV_WIDTH = 3 * NA_WIDTH + SWA_WIDTH + 2 * SWA_KV_WIDTH
N_GROUPS = 4
EXPERTS_PER_GROUP = 8
N_EXPERTS = N_GROUPS * EXPERTS_PER_GROUP
TOP_K_IN_GROUP = 2
EXPERT_FF = 256
N_MOD = 6
EPS = 1e-6
NEG_INF = -1e30

kernel_name = "hymba_na_swa_hmoe_encoder"

def rmsnorm(x, g):
    xf = x.astype(jnp.float32)
    y = xf * lax.rsqrt(jnp.mean(xf * xf, axis=-1, keepdims=True) + EPS)
    return (y * g.astype(jnp.float32)).astype(x.dtype)

def rope(x, pos):
    d = x.shape[-1]
    half = d // 2
    inv = ROPE_THETA ** (-jnp.arange(half, dtype=jnp.float32) * 2.0 / d)
    ang = pos.astype(jnp.float32)[:, None] * inv[None, :]
    cos = jnp.cos(ang)[None, :, None, :]
    sin = jnp.sin(ang)[None, :, None, :]
    xf = x.astype(jnp.float32)
    x1, x2 = xf[..., :half], xf[..., half:]
    return jnp.concatenate([x1 * cos - x2 * sin, x2 * cos + x1 * sin], axis=-1).astype(x.dtype)

def neighborhood_attention(q, k, v, rpb):
    b, s, h, d = q.shape
    rows = s // GRID_W
    kh = min(NA_KH_MAX, rows)
    qg = q.reshape(b, rows, GRID_W, h, d)
    kg = k.reshape(b, rows, GRID_W, h, d)
    vg = v.reshape(b, rows, GRID_W, h, d)
    col = jnp.arange(GRID_W)
    col_start = jnp.clip(col - NA_KW // 2, 0, GRID_W - NA_KW)
    col_idx = col_start[:, None] + jnp.arange(NA_KW)[None, :]
    dc = col_idx - col[:, None] + (NA_KW - 1)
    scale = d ** -0.5

    def row_block(r):
        r0 = jnp.clip(r - kh // 2, 0, rows - kh)
        k_rows = lax.dynamic_slice_in_dim(kg, r0, kh, axis=1)
        v_rows = lax.dynamic_slice_in_dim(vg, r0, kh, axis=1)
        k_win = k_rows[:, :, col_idx]
        v_win = v_rows[:, :, col_idx]
        q_row = lax.dynamic_index_in_dim(qg, r, axis=1, keepdims=False)
        dr = r0 + jnp.arange(kh) - r + (NA_KH_MAX - 1)
        bias = rpb[:, dr[:, None, None], dc[None, :, :]]
        bias = jnp.transpose(bias, (0, 2, 1, 3)).astype(jnp.float32)
        logits = jnp.einsum('bqhd,biqjhd->bhqij', q_row, k_win).astype(jnp.float32) * scale
        logits = logits + bias[None]
        p = jax.nn.softmax(logits.reshape(b, h, GRID_W, kh * NA_KW), axis=-1)
        p = p.reshape(b, h, GRID_W, kh, NA_KW).astype(v.dtype)
        return jnp.einsum('bhqij,biqjhd->bqhd', p, v_win)

    out = lax.map(row_block, jnp.arange(rows))
    return jnp.transpose(out, (1, 0, 2, 3, 4)).reshape(b, s, h * d)

def sliding_window_gqa(q, k, v, sinks):
    b, s, hq, d = q.shape
    hkv = k.shape[2]
    g = hq // hkv
    nb = s // SWA_BLOCK
    qb = q.reshape(b, nb, SWA_BLOCK, hkv, g, d)

    def band(t):
        tp = jnp.pad(t, ((0, 0), (SWA_BLOCK, SWA_BLOCK), (0, 0), (0, 0)))
        tb = tp.reshape(b, nb + 2, SWA_BLOCK, hkv, d)
        return jnp.concatenate([tb[:, :-2], tb[:, 1:-1], tb[:, 2:]], axis=2)

    kb, vb = band(k), band(v)
    q_off = jnp.arange(SWA_BLOCK)
    k_off = jnp.arange(3 * SWA_BLOCK) - SWA_BLOCK
    in_window = jnp.abs(k_off[None, :] - q_off[:, None]) <= SWA_WINDOW
    k_abs = jnp.arange(nb)[:, None] * SWA_BLOCK + k_off[None, :]
    k_valid = (k_abs >= 0) & (k_abs < s)
    mask = in_window[None] & k_valid[:, None, :]
    logits = jnp.einsum('bnqhgd,bnkhd->bnhgqk', qb, kb).astype(jnp.float32) * (d ** -0.5)
    logits = jnp.where(mask[None, :, None, None], logits, NEG_INF)
    sink = jnp.broadcast_to(sinks.astype(jnp.float32).reshape(hkv, g)[None, None, :, :, None, None],
                            logits.shape[:-1] + (1,))
    p = jax.nn.softmax(jnp.concatenate([logits, sink], axis=-1), axis=-1)[..., :-1]
    out = jnp.einsum('bnhgqk,bnkhd->bnqhgd', p.astype(v.dtype), vb)
    return out.reshape(b, s, hq * d)

def hierarchical_moe(h, w_group_router, w_expert_router, w_gate, w_up, w_down):
    b, s, d = h.shape
    n = b * s
    t = h.reshape(n, d)
    g_logits = (t @ w_group_router).astype(jnp.float32)
    g_probs = jax.nn.softmax(g_logits, axis=-1)
    g_top = jnp.argmax(g_logits, axis=-1)
    g_weight = jnp.take_along_axis(g_probs, g_top[:, None], axis=-1)
    e_logits = jnp.einsum('nd,gde->nge', t, w_expert_router).astype(jnp.float32)
    e_in = jnp.take_along_axis(e_logits, g_top[:, None, None], axis=1)[:, 0]
    top_vals, top_idx = lax.top_k(e_in, TOP_K_IN_GROUP)
    top_w = jax.nn.softmax(top_vals, axis=-1) * g_weight
    expert_id = g_top[:, None] * EXPERTS_PER_GROUP + top_idx
    gates = jnp.sum(jax.nn.one_hot(expert_id, N_EXPERTS, dtype=jnp.float32) * top_w[..., None], axis=1)
    y = jnp.zeros((n, d), jnp.float32)
    for e in range(N_EXPERTS):
        he = jax.nn.silu(t @ w_gate[e]) * (t @ w_up[e])
        y = y + gates[:, e:e + 1] * (he @ w_down[e]).astype(jnp.float32)
    return y.astype(h.dtype).reshape(b, s, d)

def setup_inputs(seed: int = 0) -> dict:
    key = jax.random.key(seed)
    ks = jax.random.split(key, 20)
    f32 = jnp.float32
    nrm = lambda k, shape, sc: jax.random.normal(k, shape, f32) * sc
    return {
        "x": nrm(ks[0], (BATCH, SEQ, D_MODEL), 1.0),
        "c": nrm(ks[1], (BATCH, D_MODEL), 1.0),
        "w_ada": nrm(ks[2], (DEPTH, D_MODEL, N_MOD * D_MODEL), 0.5 * D_MODEL ** -0.5),
        "b_ada": nrm(ks[3], (DEPTH, N_MOD * D_MODEL), 0.01),
        "g_pre_mix": 1.0 + nrm(ks[4], (DEPTH, D_MODEL), 0.02),
        "w_in": nrm(ks[5], (DEPTH, D_MODEL, QKV_WIDTH), D_MODEL ** -0.5),
        "na_rpb": nrm(ks[6], (DEPTH, NA_HEADS, 2 * NA_KH_MAX - 1, 2 * NA_KW - 1), 0.1),
        "swa_sinks": nrm(ks[7], (DEPTH, SWA_HEADS), 1.0),
        "beta_na": 1.0 + nrm(ks[8], (DEPTH, NA_WIDTH), 0.02),
        "beta_swa": 1.0 + nrm(ks[9], (DEPTH, SWA_WIDTH), 0.02),
        "w_out": nrm(ks[10], (DEPTH, MIX_WIDTH, D_MODEL), MIX_WIDTH ** -0.5),
        "g_post_mix": 1.0 + nrm(ks[11], (DEPTH, D_MODEL), 0.02),
        "g_pre_ffn": 1.0 + nrm(ks[12], (DEPTH, D_MODEL), 0.02),
        "w_group_router": nrm(ks[13], (DEPTH, D_MODEL, N_GROUPS), D_MODEL ** -0.5),
        "w_expert_router": nrm(ks[14], (DEPTH, N_GROUPS, D_MODEL, EXPERTS_PER_GROUP), D_MODEL ** -0.5),
        "w_gate": nrm(ks[15], (DEPTH, N_EXPERTS, D_MODEL, EXPERT_FF), D_MODEL ** -0.5),
        "w_up": nrm(ks[16], (DEPTH, N_EXPERTS, D_MODEL, EXPERT_FF), D_MODEL ** -0.5),
        "w_down": nrm(ks[17], (DEPTH, N_EXPERTS, EXPERT_FF, D_MODEL), EXPERT_FF ** -0.5),
        "g_post_ffn": 1.0 + nrm(ks[18], (DEPTH, D_MODEL), 0.02),
    }

def reference(x, c, w_ada, b_ada, g_pre_mix, w_in, na_rpb, swa_sinks, beta_na, beta_swa,
              w_out, g_post_mix, g_pre_ffn, w_group_router, w_expert_router, w_gate, w_up,
              w_down, g_post_ffn):
    b, s, d = x.shape
    pos = jnp.arange(s)
    o_nq, o_nk, o_nv = 0, NA_WIDTH, 2 * NA_WIDTH
    o_sq = 3 * NA_WIDTH
    o_sk = o_sq + SWA_WIDTH
    o_sv = o_sk + SWA_KV_WIDTH
    for l in range(DEPTH):
        mod = (jax.nn.silu(c) @ w_ada[l] + b_ada[l]).reshape(b, N_MOD, d)
        shift_a, scale_a, gate_a = mod[:, 0, None], mod[:, 1, None], mod[:, 2, None]
        shift_f, scale_f, gate_f = mod[:, 3, None], mod[:, 4, None], mod[:, 5, None]

        h = rmsnorm(x, g_pre_mix[l]) * (1.0 + scale_a) + shift_a
        qkv = h @ w_in[l]
        na_q = qkv[..., o_nq:o_nk].reshape(b, s, NA_HEADS, HEAD_DIM)
        na_k = qkv[..., o_nk:o_nv].reshape(b, s, NA_HEADS, HEAD_DIM)
        na_v = qkv[..., o_nv:o_sq].reshape(b, s, NA_HEADS, HEAD_DIM)
        sw_q = rope(qkv[..., o_sq:o_sk].reshape(b, s, SWA_HEADS, HEAD_DIM), pos)
        sw_k = rope(qkv[..., o_sk:o_sv].reshape(b, s, SWA_KV_HEADS, HEAD_DIM), pos)
        sw_v = qkv[..., o_sv:].reshape(b, s, SWA_KV_HEADS, HEAD_DIM)
        na_out = rmsnorm(neighborhood_attention(na_q, na_k, na_v, na_rpb[l]), beta_na[l])
        sw_out = rmsnorm(sliding_window_gqa(sw_q, sw_k, sw_v, swa_sinks[l]), beta_swa[l])
        mix = jnp.concatenate([na_out, sw_out], axis=-1) @ w_out[l]
        x = x + gate_a * rmsnorm(mix, g_post_mix[l])

        h = rmsnorm(x, g_pre_ffn[l]) * (1.0 + scale_f) + shift_f
        y = hierarchical_moe(h, w_group_router[l], w_expert_router[l], w_gate[l], w_up[l], w_down[l])
        x = x + gate_f * rmsnorm(y, g_post_ffn[l])
    return x


_drawn_inputs = setup_inputs


def setup_inputs(seed=0):
    import zlib

    import numpy as np

    out = dict(_drawn_inputs(seed))
    spreads = {}
    factors = {'swa_sinks': 8.0, 'g_post_ffn': 8.0}
    for name, (base, spread) in spreads.items():
        noise = np.random.default_rng([zlib.crc32(name.encode()), seed]).standard_normal(out[name].shape)
        drawn = base * np.exp(spread * noise) if base else spread * noise
        out[name] = __import__('jax').numpy.asarray(drawn.astype(out[name].dtype))
    for name, factor in factors.items():
        out[name] = (out[name] * factor).astype(out[name].dtype)
    return out
```

```python
import numpy as np

import concourse.bass as bass
from concourse import mybir
from concourse.alu_op_type import AluOpType as ALU
from contextlib import ExitStack

F32 = mybir.dt.float32
F32R = mybir.dt.float32r
BF16 = mybir.dt.bfloat16
U32 = mybir.dt.uint32
ACT = mybir.ActivationFunctionType
AX = mybir.AxisListType
ds = bass.ds

P = 128
S = 1024
T = S // P
D = 1024
K = D // P
GRID_W = 64
HD = 64
KH, KW = 8, 16
ROWS = S // GRID_W
NG, EPG = 4, 8
NE = NG * EPG
FF = 256
EPS = 1e-6
NEG = -1e30
CH = 256
N_IN = 9
SLICES = 29
BIAS_PARTS = ((0, 10), (10, 19), (19, 29))
MAXB = 48
BIG_ROW = 1 << 20

C_ID, C_ONE, C_TRI, C_COS, C_SIN = 0, 128, 256, 384, 384 + 512
C_SWM = 384 + 1024
C_NAM = C_SWM + 384
C_SEL = C_NAM + 64
C_IOTA = C_SEL + 256
C_STEP = C_IOTA + 48
C_ODD = C_STEP + 8
C_TOK = C_ODD + 8
C_RQ0, C_RQ1, C_EPS = C_TOK + 16, C_TOK + 17, C_TOK + 18
C_PLUS = C_TOK + 19
C_HEAD = C_PLUS + 4
C_END = C_PLUS + 6

R_A, R_C, R_O = 0, 256, 544
R_EM, R_G, R_V, R_T, R_M = 1056, 1312, 1376, 1440, 1952
R_EI, R_EX = 2240, 2280
R_OG, R_GI, R_GW, R_W, R_ID, R_P, R_B, R_OS, R_GE = (2320 + x for x in (0, 32, 40, 48, 64, 80, 96, 112, 128))
R_OB, R_OC, R_OX, R_BT, R_END = 1056, 1088, 1120, 1152, 2464

V_BADA, V_G, V_BETA, V_C = 0, 16, 24, 32
V_END = 40


def na_window(a):
    r0 = min(max(2 * a - KH // 2, 0), ROWS - KH)
    r1 = min(max(2 * a + 1 - KH // 2, 0), ROWS - KH)
    n = r1 + KH - r0
    if n == KH + 1:
        return r0, n, 10
    return r0, n, r0 - 2 * a + (2 if a < 2 else 25)


def bc(ap, axis, n):
    shape = list(ap.shape)
    shape[axis] = n
    return ap.broadcast_to(shape)


def sw_window(b):
    lo, hi = max(b - 1, 0), min(b + 1, T - 1)
    return lo, hi - lo + 1, lo - b + 1


def build(nc, x, consts, vecs, b_rows, g_rows, rpb_cols, sinks, w_ada, w_in, w_out, w_router, w_gu, w_down, out):
    BASE = 16512

    def sbt(name, shape, dt, kb):
        return nc.alloc_sbuf_tensor_at(name, shape, dt, offset=int(kb * 1024) + BASE)

    with ExitStack() as ctx:
        def sem(name):
            return ctx.enter_context(nc.semaphore(name))

        kt = sbt("kt", [P, C_END], F32, 0)
        vt = sbt("vt", [P, V_END], F32, 8.75)
        nsink = sbt("nsink", [P, 8], F32, 8.9375)
        small = sbt("small", [P, 240], F32, 9)
        svt = sbt("svt", [P, T, P], F32, 194)
        vna = sbt("vna", [P, T, 512], F32, 10)
        rcol = sbt("rcol", [63, 112], F32, 22.0)
        junk_x = sbt("junk_x", [P, D], BF16, 22.5)
        junk = sbt("junk", [P, D], BF16, 198)
        acc_a = sbt("acc_a", [P, 8, CH], F32, 58)
        adaA = [sbt(f"adaA{i}", [P, K, CH], F32, 106 + 8 * i) for i in range(4)]
        xs = sbt("xs", [P, T, D], F32, 138)
        bias_b = sbt("bias_b", [P, 16, 8, 64], F32, 170)
        hf = [sbt(f"hf{i}", [P, 512], F32, 202 + 2 * i) for i in range(2)]
        hh = sbt("hh", [P, K, S], F32R, 26)
        hl = sbt("hl", [P, K, S], F32R, 58)
        wf = [sbt(f"wf{i}", [P, K, CH], F32, 90 + 8 * i) for i in range(2)]
        wh = [sbt(f"wh{i}", [P, K, CH], F32R, 106 + 16 * i) for i in range(2)]
        wl = [sbt(f"wl{i}", [P, K, CH], F32R, 114 + 16 * i) for i in range(2)]
        tmq = sbt("tmq", [P, T, 512], F32, 154)
        tmk = sbt("tmk", [P, T, 256], F32, 178)
        rt1 = sbt("rt1", [P, CH], F32, 202)
        rt2 = sbt("rt2", [P, CH], F32, 203)
        qall = sbt("qall", [P, 8, S], F32, 138)
        kall = sbt("kall", [P, 6, S], F32, 170)
        ot = sbt("ot", [P, T, D], F32, 26)
        adaC = [sbt(f"adaC{i}", [P, K, CH], F32, 58 + 8 * i) for i in range(2)]
        mods = sbt("mods", [P, 4, D], F32, 74)
        bias = sbt("bias", [P, SLICES, P], F32, 106)
        acc_c = sbt("acc_c", [P, 2, CH], F32, 90)
        b_row = sbt("b_row", [1, 512], F32, 92)
        beta_b = sbt("beta_b", [P, D], F32, 200)
        qz = sbt("qz", [P, 2, S], F32, 94)
        ks = sbt("ks", [P, S], F32, 102)
        pb = [sbt(f"pb{i}", [P, 576], F32, 122 + 2.25 * i) for i in range(4)]
        pt = [sbt(f"pt{i}", [P, 640], F32, 131 + 2.5 * i) for i in range(2)]
        asm = sbt("asm", [P, 128], F32, 136)
        WO = (138, 146, 170, 58)
        wof = [sbt(f"wof{i}", [P, K, CH], F32, WO[i]) for i in range(4)]
        wol = [sbt(f"wol{i}", [P, K, CH], F32R, WO[i]) for i in range(4)]
        woh = [sbt(f"woh{i}", [P, K, CH], F32R, (154, 162, 178, 186)[i]) for i in range(4)]
        mh = [sbt(f"mh{i}", [P, K, P], F32R, (106, 98)[i]) for i in range(2)]
        ml = [sbt(f"ml{i}", [P, K, P], F32R, (110, 102)[i]) for i in range(2)]
        osc = sbt("osc", [P, D], F32, 114)
        xb = [sbt(f"xb{i}", [P, D], F32, 118 + 4 * i) for i in range(2)]
        h2 = [sbt(f"h2{i}", [P, D], F32, 126 + 4 * i) for i in range(2)]
        h2T = sbt("h2T", [P, K, P], F32, 70)
        x1 = sbt("x1", [P, T, D], F32, 26)
        lg = sbt("lg", [P, T, 36], F32, 136.75)
        wrt = sbt("wrt", [P, K, 36], F32, 66)
        rw = sbt("rw", [P, 2560], F32, 90)
        ridx = sbt("ridx", [P, 16], U32, 100.25)
        rec = sbt("rec", [P, 16, 4], U32, 100.5)
        btab = sbt("btab", [P, 64], U32, 100.75)
        ru = sbt("ru", [P, 128], U32, 101)
        tab = sbt("tab", [P, MAXB, 4], U32, 204)
        ixg = [sbt(f"ixg{i}", [P, 1], U32, 206 + 0.0625 * i) for i in range(2)]
        ixs = [sbt(f"ixs{i}", [P, 1], U32, 206.125 + 0.0625 * i) for i in range(2)]
        wgu = [sbt(f"wgu{i}", [P, K, 512], F32, 138 + 16 * i) for i in range(2)]
        wd = [sbt(f"wd{i}", [P, 2, D], F32, 170 + 8 * i) for i in range(2)]
        xg = [sbt(f"xg{i}", [P, D], F32, 106 + 4 * i) for i in range(2)]
        xgT = [sbt(f"xgT{i}", [P, K, P], F32, 114 + 4 * i) for i in range(2)]
        sg = [sbt(f"sg{i}", [P, FF], F32, 122 + i) for i in range(2)]
        hid = [sbt(f"hid{i}", [P, FF], F32, 124 + i) for i in range(2)]
        hidT = [sbt(f"hidT{i}", [P, 2, P], F32, 126 + i) for i in range(2)]
        yg = [sbt(f"yg{i}", [P, D], F32, 128 + 4 * i) for i in range(2)]
        ya = [sbt(f"ya{i}", [P, D], F32, 90 + 4 * i) for i in range(2)]
        yb = [sbt(f"yb{i}", [P, D], F32, 106 + 4 * i) for i in range(2)]
        yo = [sbt(f"yo{i}", [P, D], F32, 114 + 4 * i) for i in range(2)]
        ps = ctx.enter_context(nc.psum_tensor("ps", [P, 8, 512], F32))

        ident, ones, tri = kt[:, C_ID:C_ID + P], kt[:, C_ONE:C_ONE + P], kt[:, C_TRI:C_TRI + P]
        eps = kt[:, C_EPS:C_EPS + 1]
        col_scale, col_shift = small[:, 0:8], small[:, 8:16]
        xss, xrt, xrs = small[:, 16:24], small[:, 24:32], small[:, 32:40]
        oss, ort, ors = small[:, 40:56], small[:, 56:72], small[:, 72:88]
        csil = small[:, 88:96]
        mst, gst, fst = small[:, 96:120], small[:, 120:144], small[:, 144:168]
        mcol = small[:, 168:184]

        def banks(b, n=2):
            return ps[:, b:b + n, :].rearrange("p b n -> p (b n)")

        bias_dram = nc.dram_tensor("bias_dram", [4, P, SLICES, P], F32).ap()
        h2_dram = nc.dram_tensor("h2_dram", [S, D], F32).ap()
        tab_dram = nc.dram_tensor("tab_dram", [P * MAXB, 4], U32).ap()
        y2_dram = nc.dram_tensor("y2_dram", [2 * S, D], F32).ap()

        const_in, vec_in, x_in = sem("const_in"), sem("vec_in"), [sem(f"x_in{i}") for i in range(2)]
        ada_in = [sem(f"ada_in{i}") for i in range(4)]
        ada_acc, csil_ok, bias_mm, bias_ev, bias_spec = sem("ada_acc"), sem("csil_ok"), sem("bias_mm"), sem("bias_ev"), sem("bias_spec")
        modcol_mm, cols_ok, bias_saved = sem("modcol_mm"), sem("cols_ok"), sem("bias_saved")
        squared, x_root, x_scaled, xT_mm, xT_f, h_split = (sem(n) for n in ("squared", "x_root", "x_scaled", "xT_mm", "xT_f", "h_split"))
        win_in, win_hi, win_lo = [sem(f"win_in{i}") for i in range(2)], sem("win_hi"), sem("win_lo")
        proj_mm, proj_out, swT_mm, swT_ev, dve_chain = (sem(n) for n in ("proj_mm", "proj_out", "swT_mm", "swT_ev", "dve_chain"))
        bias_in, adaC_in, rows_in, brow_in = [sem(f"bias_in{i}") for i in range(3)], [sem(f"adaC_in{i}") for i in range(2)], sem("rows_in"), sem("brow_in")
        stage_due = sem("stage_due")
        staged, pt_half = sem("staged"), sem("pt_half")
        qk_mm, logits_ok, exp_ok, pT_mm, pt_ok, pv_mm, o_ok = (
            sem(n) for n in ("qk_mm", "logits_ok", "exp_ok", "pT_mm", "pt_ok", "pv_mm", "o_ok"))
        adaC_used, mod_mm, mod_ok = (sem(n) for n in ("adaC_used", "mod_mm", "mod_ok"))
        o_root, logits_due, ix_due = sem("o_root"), sem("logits_due"), sem("ix_due")
        wout_in, beta_in, wout_hi, wout_lo, router_in = [sem(f"wout_in{i}") for i in range(4)], sem("beta_in"), sem("wout_hi"), sem("wout_lo"), sem("router_in")
        os_ok, oT_mm, m_hi, m_lo, mix_mm, mix_root, x1_ok, x1_root = (
            sem(n) for n in ("os_ok", "oT_mm", "m_hi", "m_lo", "mix_mm", "mix_root", "x1_ok", "x1_root"))
        xb_in = [sem(f"xb_in{i}") for i in range(2)]
        h2_ok, h2_saved = sem("h2_ok"), [sem(f"h2_saved{i}") for i in range(2)]
        h2T_mm, h2T_ok, lg_mm, lg_ok = (sem(n) for n in ("h2T_mm", "h2T_ok", "lg_mm", "lg_ok"))
        r_exp, r_pre, pos_mm, r_exp_in, tab_init, tab_fill = (sem(n) for n in ("r_exp", "r_pre", "pos_mm", "r_exp_in", "tab_init", "tab_fill"))
        rec_ok, tab_put, tab_in, np_ok = (sem(n) for n in ("rec_ok", "tab_put", "tab_in", "np_ok"))
        gu_in, dn_in = [sem(f"gu_in{i}") for i in range(2)], [sem(f"dn_in{i}") for i in range(2)]
        ix_ok, xg_in, xg_zero = sem("ix_ok"), [sem(f"xg_in{i}") for i in range(2)], sem("xg_zero")
        xgT_mm, xgT_a, xgT_b, gu_mm, sg_ok, hid_ok, hidT_mm, hidT_ok, dn_mm, yg_a, yg_b = (
            sem(n) for n in ("xgT_mm", "xgT_a", "xgT_b", "gu_mm", "sg_ok", "hid_ok", "hidT_mm", "hidT_ok", "dn_mm", "yg_a", "yg_b"))
        y_put = [sem(f"y_put{i}") for i in range(2)]
        moe_done, ya_in, yb_in = sem("moe_done"), [sem(f"ya_in{i}") for i in range(2)], [sem(f"yb_in{i}") for i in range(2)]
        y_sum, y_root, yo_ok = (sem(n) for n in ("y_sum", "y_root", "yo_ok"))
        out_put = [sem(f"out_put{i}") for i in range(2)]

        def na_win(a):
            r0, n, _ = na_window(a)
            return GRID_W * r0, GRID_W * n

        def sw_win(b):
            lo, n, _ = sw_window(b)
            return P * lo, P * n

        def tiles(window, a):
            first, width = window(a)
            return range(first // P, -(-(first + width) // P))

        def staging(window):
            return [(kind, t, a) for a in range(T) for kind in (0, 1, "k") for t in range(T)
                    if a == (max(b for b in range(T) if t in tiles(window, b)) if kind == "k" else t)]

        def needed(window, orders, a):
            want = {(0, a), (1, a)} | {("k", t) for t in tiles(window, a)}
            return max(max(i for i, (kind, t, _) in enumerate(o) if (kind, t) in want) + 1 for o in orders)

        STAGE_SW, STAGE_NA = staging(sw_win), staging(na_win)
        STEPS = len(STAGE_SW)
        mod_bank = lambda window: ps[:, 1 if window is sw_win else 5, :]
        T_bank = lambda n, nb: 4 + (n % 2 if nb <= 3 else 0)
        on_dve = lambda n, slides: not slides and n % 4 == 3

        block = ctx.enter_context(nc.Block())

        @block.sync
        def _(sp):
            sp.dma_start(kt[:, :], consts).then_inc(const_in, 16)
            sp.dma_start(vt[:, :], vecs).then_inc(vec_in, 16)
            sp.dma_start(rcol[:, :], rpb_cols).then_inc(vec_in, 16)
            sp.dma_start(nsink[:, :], sinks[0:1, :].broadcast_to([P, 8])).then_inc(vec_in, 16)
            for i in range(2):
                sp.dma_start(xs[:, 4 * i:4 * i + 4, :],
                             x[512 * i:512 * i + 512, :].rearrange("(t p) d -> p t d", p=P)).then_inc(x_in[i], 16)
            for i in range(4):
                sp.dma_start(adaA[i][:, :, :], w_ada[i]).then_inc(ada_in[i], 16)
            for i in range(4):
                sp.wait_ge(ada_acc, i + 1)
                sp.dma_start(adaA[i][:, :, :], w_ada[4 + i]).then_inc(ada_in[i], 16)
            for i in range(2):
                sp.dma_start(wf[i][:, :, :], w_in[i]).then_inc(win_in[i], 16)
            sp.wait_ge(bias_spec, 1)
            for hp in range(4):
                pair = bias_b[:, :, 2 * hp:2 * hp + 2, :].rearrange("p m h c -> p m (h c)")
                for dst, src, n in ((0, 4, 10), (10, 14, 1), (11, 3, 7), (18, 15, 1), (19, 0, 10)):
                    sp.dma_start(bias_dram[hp, :, dst:dst + n, :], pair[:, src:src + n, :]).then_inc(bias_saved, 16)
            for n in range(2, N_IN):
                sp.wait_ge(win_hi, n - 1)
                sp.wait_ge(win_lo, n - 1)
                sp.dma_start(wf[n % 2][:, :, :], w_in[n]).then_inc(win_in[n % 2], 16)
            sp.wait_ge(bias_saved, 16 * 20)
            sp.wait_ge(proj_mm, 56)
            for i in range(3):
                sp.dma_start(mods[:, (0, 2, 3)[i], :], g_rows[i:i + 1, :].broadcast_to([P, D])).then_inc(rows_in, 16)
            sp.dma_start(b_row[:, :], b_rows[0:1, :]).then_inc(brow_in, 16)
            for i in range(2):
                sp.dma_start(adaC[i][:, :, :], w_ada[8 + i]).then_inc(adaC_in[i], 16)
            for i, (s0, s1) in enumerate(BIAS_PARTS):
                sp.dma_start(bias[:, s0:s1, :], bias_dram[0, :, s0:s1, :]).then_inc(bias_in[i], 16)
            sp.dma_start(beta_b[:, :], g_rows[3:4, :].broadcast_to([P, D])).then_inc(beta_in, 16)

            def next_ada(i, pair):
                sp.wait_ge(adaC_used, 2 * pair + (i + 1))
                sp.dma_start(adaC[i][:, :, :], w_ada[ds(2 * pair + (10 + i), 1)].rearrange("a p k n -> (a p) k n")).then_inc(adaC_in[i], 16)

            def next_b(pair):
                sp.wait_ge(mod_mm, pair + 1)
                sp.dma_start(b_row[:, :], b_rows[ds(pair + 1, 1), :]).then_inc(brow_in, 16)

            def next_bias(i, hp, tile):
                s0, s1 = BIAS_PARTS[i]
                sp.wait_ge(logits_ok, 16 * hp + (64 + 2 * tile + 2))
                sp.dma_start(bias[:, s0:s1, :], bias_dram[ds(hp + 1, 1), :, s0:s1, :].rearrange("a p s n -> (a p) s n")).then_inc(bias_in[i], 16)

            with sp.Fori(0, 4) as hp:
                next_ada(0, hp)
                next_ada(1, hp)
                next_b(hp)
            sp.wait_ge(staged, 5 * STEPS)
            for n in range(3):
                sp.dma_start(wof[n][:, :, :], w_out[n]).then_inc(wout_in[n], 16)
            with sp.Fori(0, 3) as hp:
                next_bias(0, hp, 1)
                next_ada(0, hp + 4)
                next_bias(1, hp, 5)
                next_ada(1, hp + 4)
                next_b(hp + 4)
                next_bias(2, hp, 7)
            sp.wait_ge(adaC_used, 15)
            sp.dma_start(wof[3][:, :, :], w_out[3]).then_inc(wout_in[3], 16)
            sp.wait_ge(adaC_used, 16)
            sp.dma_start(wrt[:, :, :], w_router).then_inc(router_in, 16)
            sp.wait_ge(tab_fill, 1)
            sp.dma_start(tab_dram.rearrange("(p b) c -> p b c", p=P), tab[:, :, :]).then_inc(tab_init, 16)
            for t in range(T):
                if t == 0:
                    sp.wait_ge(pv_mm, 128)
                if t >= 2:
                    sp.wait_ge(x1_ok, t - 1)
                sp.dma_start(xb[t % 2][:, :], x[P * t:P * t + P, :]).then_inc(xb_in[t % 2], 16)
                if t >= 1:
                    sp.wait_ge(h2_ok, t)
                    sp.dma_start(h2_dram[P * t - P:P * t, :], h2[(t - 1) % 2][:, :]).then_inc(h2_saved[(t - 1) % 2], 16)
            sp.wait_ge(h2_ok, T)
            sp.dma_start(h2_dram[P * T - P:P * T, :], h2[(T - 1) % 2][:, :]).then_inc(h2_saved[(T - 1) % 2], 16)
            sp.wait_ge(mix_mm, T)
            for i in range(2):
                sp.dma_start(wgu[i][:, :, :], w_gu[i]).then_inc(gu_in[i], 16)
                sp.dma_start(wd[i][:, :, :], w_down[i]).then_inc(dn_in[i], 16)
            sp.wait_ge(tab_put, 16 * 16)
            sp.dma_start(tab[:, :, :], tab_dram.rearrange("(p b) c -> p b c", p=P)).then_inc(tab_in, 16)
            sp.wait_ge(np_ok, 1)
            n_pairs = sp.value_load(btab[0:1, MAXB:MAXB + 1], min_val=NE // 2 - 2, max_val=MAXB // 2 - 2) + 2

            def expert(b):
                return sp.value_load(btab[0:1, ds(b, 1)], min_val=0, max_val=NE - 1)

            def load_gu(u, b):
                e = expert(b)
                sp.wait_ge(gu_mm, b - 1)
                sp.dma_start(wgu[u][:, :, :], w_gu[ds(e, 1)].rearrange("a p k n -> (a p) k n")).then_inc(gu_in[u], 16)

            def load_dn(u, b):
                e = expert(b)
                sp.wait_ge(dn_mm, b - 1)
                sp.dma_start(wd[u][:, :, :], w_down[ds(e, 1)].rearrange("a p k n -> (a p) k n")).then_inc(dn_in[u], 16)

            load_gu(0, 2)
            with sp.Fori(1, n_pairs - 1) as j:
                for u in range(2):
                    load_gu(1 - u, 2 * j + (u + 1))
                    load_dn(u, 2 * j + u)
            load_gu(1, 2 * n_pairs - 1)
            for u in range(2):
                load_dn(u, 2 * n_pairs - 2 + u)
            sp.wait_ge(moe_done, 1)
            for t in range(T):
                if t >= 2:
                    sp.wait_ge(yo_ok, t - 1)
                sp.dma_start(ya[t % 2][:, :], y2_dram[P * t:P * t + P, :]).then_inc(ya_in[t % 2], 16)
                sp.dma_start(yb[t % 2][:, :], y2_dram[S + P * t:S + P * t + P, :]).then_inc(yb_in[t % 2], 16)
                if t >= 1:
                    sp.wait_ge(yo_ok, t)
                    sp.dma_start(out[P * t - P:P * t, :], yo[(t - 1) % 2][:, :]).then_inc(out_put[(t - 1) % 2], 16)
            sp.wait_ge(yo_ok, T)
            sp.dma_start(out[P * T - P:P * T, :], yo[(T - 1) % 2][:, :]).then_inc(out_put[(T - 1) % 2], 16)
            for i in range(2):
                sp.wait_ge(out_put[i], 16 * (T // 2))

        @block.tensor
        def _(pe):
            def three(dst, ah, al, bh, bl, first, last):
                pe.matmul(dst, ah, bh, start=first, stop=False)
                pe.matmul(dst, al, bh, start=False, stop=False)
                return pe.matmul(dst, ah, bl, start=False, stop=last)

            pe.wait_ge(const_in, 16)
            pe.wait_ge(vec_in, 48)
            for g in range(16):
                if g >= 2:
                    pe.wait_ge(bias_ev, g - 1)
                for c in range(4):
                    kc = 4 * g + c
                    sel = kt[0:63, C_SEL + 63 - kc:C_SEL + 191 - kc]
                    mm = pe.matmul(ps[:, g % 2, 112 * c:112 * c + 112], sel, rcol[:, :], start=True, stop=True)
                mm.then_inc(bias_mm, 1)
            for c in range(8):
                pe.wait_ge(ada_acc, c + 1)
                for i in range(2):
                    mm = pe.matmul(ps[:, 7, 2 * c + i:2 * c + i + 1], acc_a[:, c, P * i:P * i + P], ones[:, 0:1], start=True, stop=True)
            mm.then_inc(modcol_mm, 1)
            for g in range(16):
                if g % 8 == 0:
                    pe.wait_ge(x_scaled, 4 * (g // 8) + 4)
                if g >= 4:
                    pe.wait_ge(xT_f, g - 3)
                for q in range(4):
                    mm = pe.transpose(ps[:, 2 + g % 4, P * q:P * q + P], xs[:, 4 * (g // 8) + q, P * (g % 8):P * (g % 8) + P], ident)
                mm.then_inc(xT_mm, 1)
            pe.wait_ge(h_split, 16)

            def tokens_major(n, b, skip=0):
                pe.wait_ge(win_hi, n + 1)
                pe.wait_ge(win_lo, n + 1)
                for t in range(T):
                    if t >= skip:
                        pe.wait_ge(proj_out, 8 * n + (t - 3))
                    for k in range(K):
                        mm = three(ps[:, t % 4, 0:CH], hh[:, k, P * t:P * t + P], hl[:, k, P * t:P * t + P],
                                   wh[b][:, k, :], wl[b][:, k, :], k == 0, k == K - 1)
                    mm.then_inc(proj_mm, 1)

            tokens_major(0, 0, skip=4)
            with pe.Fori(0, 2) as i:
                for u in range(2):
                    tokens_major(2 * i + (1 + u), (1 + u) % 2)
            pe.wait_ge(proj_out, 24)
            for g in range(12):
                if g >= 4:
                    pe.wait_ge(swT_ev, g - 3)
                for q in range(4):
                    src = tmq[:, 4 * (g % 2) + q, P * (g // 2):P * (g // 2) + P] if g < 8 else tmk[:, 4 * (g % 2) + q, P * (g // 2 - 4):P * (g // 2 - 3)]
                    mm = pe.transpose(ps[:, 4 + g % 4, P * q:P * q + P], src, ident)
                mm.then_inc(swT_mm, 1)
            with pe.Fori(0, 2) as i:
                for u in range(2):
                    b = (1 + u) % 2
                    pe.wait_ge(win_hi, 2 * i + (6 + u))
                    pe.wait_ge(win_lo, 2 * i + (6 + u))
                    for g in range(4):
                        cols, toks = slice(P * (g // 2), P * (g // 2) + P), slice(512 * (g % 2), 512 * (g % 2) + 512)
                        pe.wait_ge(proj_out, 8 * i + (40 + 4 * u + g - 3))
                        for k in range(K):
                            mm = three(ps[:, g, :], wh[b][:, k, cols], wl[b][:, k, cols], hh[:, k, toks], hl[:, k, toks], k == 0, k == K - 1)
                        mm.then_inc(proj_mm, 1)

            def qk(n, u0, s0, window, orders):
                a, j = n // 2, n % 2
                first, width = window(a)
                pe.wait_ge(staged, s0 + needed(window, orders, a))
                if n >= 2 or not isinstance(u0, int) or u0 > 0:
                    pe.wait_ge(logits_ok, u0 + (n - 1))
                for c0, c1 in [(0, min(width, 512))] + [(512, width)] * (width > 512):
                    mm = pe.matmul(banks(2 * j)[:, c0:c1], qz[:, j, P * a:P * a + P], ks[:, first + c0:first + c1], start=True, stop=True)
                mm.then_inc(qk_mm, 1)

            def weigh(n, u0, hp, window, values):
                j, (first, width) = n % 2, window(n // 2)
                nb = -(-width // P)
                pe.wait_ge(pt_ok, u0 + (n + 1))
                if n >= 2 or not isinstance(u0, int) or u0 > 0:
                    pe.wait_ge(o_ok, u0 + (n - 1))
                for i in range(nb):
                    w = min(P, width - P * i)
                    mm = pe.matmul(ps[:, 6 + j, 0:HD], pt[j][0:w, P * i:P * i + P], values(hp, first // P + i, j, w),
                                   start=(i == 0), stop=(i == nb - 1))
                mm.then_inc(pv_mm, 1)

            def attention(pair, hp, window, values, orders, ahead, before):
                u0, s0 = 16 * pair, STEPS * pair
                for n in range(16):
                    width = window(n // 2)[1]
                    nb = -(-width // P)
                    pe.wait_ge(exp_ok, u0 + (n + 1))
                    turns = 2 if nb <= 3 else 1
                    if n >= turns or before:
                        pe.wait_ge(pt_ok, u0 + (n + 1 - turns))
                    for i in range(nb):
                        w = min(P, width - P * i)
                        mm = pe.transpose(ps[0:w, T_bank(n, nb) + i // 4, P * (i % 4):P * (i % 4) + P], pb[n % 4][:, P * i:P * i + w], ident)
                    mm.then_inc(pT_mm, 1)
                    if n + 2 < 16:
                        qk(n + 2, u0, s0, window, orders)
                    elif ahead:
                        qk(n - 14, u0 + 16, s0 + STEPS, *ahead)
                    if n >= 1:
                        weigh(n - 1, u0, hp, window, values)
                    elif before:
                        weigh(15, u0 - 16, *before)
                    if n == 15:
                        pe.wait_ge(adaC_used, 2 * pair + 2)
                        pe.wait_ge(brow_in, 16 * pair + 16)
                        pe.matmul(mod_bank(window), ones, acc_c[:, :, :].rearrange("p c n -> p (c n)"), start=True, stop=False)
                        pe.matmul(mod_bank(window), ones[0:1, :], b_row[0:1, :], start=False, stop=True).then_inc(mod_mm, 1)

            def sw_values(hp, t, j, w):
                return svt[0:w, t, ds(HD * (hp // 2), HD)]

            def na_values(hp, t, j, w):
                return vna[0:w, t, ds(P * hp + HD * j, HD)]

            pe.wait_ge(proj_out, 56)
            for n in range(2):
                qk(n, 0, 0, sw_win, [STAGE_SW])
            SW, NA = (sw_win, [STAGE_SW]), (na_win, [STAGE_SW, STAGE_NA])
            sw, na = (sw_win, sw_values), (na_win, na_values)
            attention(0, 0, *sw, [STAGE_SW], SW, None)
            with pe.Fori(1, 3) as hp:
                attention(hp, hp, *sw, [STAGE_SW], SW, (hp - 1, *sw))
            attention(3, 3, *sw, [STAGE_SW], NA, (2, *sw))
            attention(4, 0, *na, NA[1], NA, (3, *sw))
            with pe.Fori(1, 3) as hp:
                attention(hp + 4, hp, *na, NA[1], NA, (hp - 1, *na))
            attention(7, 3, *na, NA[1], None, (2, *na))
            weigh(15, 112, 3, *na)
            pe.wait_ge(o_ok, 128)
            pe.wait_ge(mod_ok, 8)

            def o_transposes(t):
                pe.wait_ge(os_ok, t + 1)
                if t >= 1:
                    pe.wait_ge(m_hi, t)
                    pe.wait_ge(m_lo, t)
                for k in range(K):
                    mm = pe.transpose(ps[:, k // 4, P * (k % 4):P * (k % 4) + P], osc[:, P * k:P * k + P], ident)
                mm.then_inc(oT_mm, 1)

            def h2_transposes(t):
                pe.wait_ge(h2_ok, t + 1)
                for k in range(K):
                    mm = pe.transpose(ps[:, 4 + k // 4, P * (k % 4):P * (k % 4) + P], h2[t % 2][:, P * k:P * k + P], ident)
                mm.then_inc(h2T_mm, 1)

            def logits(t):
                pe.wait_ge(h2T_ok, t + 1)
                if t >= 1:
                    pe.wait_ge(lg_ok, t)
                for k in range(K):
                    mm = pe.matmul(ps[:, 6, 0:36], h2T[:, k, :], wrt[:, k, :], start=(k == 0), stop=(k == K - 1))
                mm.then_inc(lg_mm, 1)

            o_transposes(0)
            pe.wait_ge(router_in, 16)
            for t in range(T):
                pe.wait_ge(m_hi, t + 1)
                pe.wait_ge(m_lo, t + 1)
                if t + 1 < T:
                    o_transposes(t + 1)
                if t >= 1:
                    pe.wait_ge(x1_ok, t)
                for c in range(4):
                    if t == 0:
                        pe.wait_ge(wout_hi, c + 1)
                        pe.wait_ge(wout_lo, c + 1)
                    for k in range(K):
                        mm = three(ps[:, 2 + c // 2, CH * (c % 2):CH * (c % 2) + CH], mh[t % 2][:, k, :], ml[t % 2][:, k, :],
                                   woh[c][:, k, :], wol[c][:, k, :], k == 0, k == K - 1)
                mm.then_inc(mix_mm, 1)
                if t >= 2:
                    logits(t - 2)
                if t >= 1:
                    h2_transposes(t - 1)
            logits(T - 2)
            h2_transposes(T - 1)
            logits(T - 1)

            pe.wait_ge(r_pre, 1)
            for t in range(T):
                pe.matmul(ps[:, 7, 32 * t:32 * t + 32], tri, rw[:, R_A + 32 * t:R_A + 32 * t + 32], start=True, stop=False)
                pe.matmul(ps[:, 7, 32 * t:32 * t + 32], ones, rw[:, R_C + 32 * t:R_C + 32 * t + 32], start=False, stop=True)
            pe.matmul(ps[:, 7, 256:288], ones, rw[:, R_C + 256:R_C + 288], start=True, stop=True).then_inc(pos_mm, 1)

            pe.wait_ge(np_ok, 1)
            n_pairs = pe.value_load(btab[0:1, MAXB:MAXB + 1], min_val=NE // 2 - 2, max_val=MAXB // 2 - 2) + 2

            def x_T(u, b, landed):
                pe.wait_ge(xg_in[u], landed)
                pe.wait_ge(xgT_a, b)
                pe.wait_ge(xgT_b, b)
                for k in range(K):
                    mm = pe.transpose(ps[:, 2 + k // 4, P * (k % 4):P * (k % 4) + P], xg[u][:, P * k:P * k + P], ident)
                mm.then_inc(xgT_mm, 1)

            def gate_up(u, b, landed, used):
                pe.wait_ge(xgT_a, b + 1)
                pe.wait_ge(xgT_b, b + 1)
                pe.wait_ge(gu_in[u], landed)
                pe.wait_ge(hid_ok, used)
                for k in range(K):
                    mm = pe.matmul(ps[:, u, :], xgT[u][:, k, :], wgu[u][:, k, :], start=(k == 0), stop=(k == K - 1))
                mm.then_inc(gu_mm, 1)

            def hid_T(u, b):
                pe.wait_ge(hid_ok, b + 1)
                pe.wait_ge(hidT_ok, b)
                for k in range(2):
                    mm = pe.transpose(ps[:, 4, P * k:P * k + P], hid[u][:, P * k:P * k + P], ident)
                mm.then_inc(hidT_mm, 1)

            def down(u, b, landed):
                pe.wait_ge(hidT_ok, b + 1)
                pe.wait_ge(dn_in[u], landed)
                pe.wait_ge(yg_a, b)
                pe.wait_ge(yg_b, b)
                for i in range(2):
                    for k in range(2):
                        mm = pe.matmul(ps[:, 5 + i, :], hidT[u][:, k, :], wd[u][:, k, 512 * i:512 * i + 512], start=(k == 0), stop=(k == 1))
                mm.then_inc(dn_mm, 1)

            x_T(0, 0, 16)
            gate_up(0, 0, 16, 0)
            x_T(1, 1, 16)
            with pe.Fori(1, n_pairs) as j:
                for u in (1, 0):
                    b = 2 * j - u
                    gate_up(u, b, 16 * j + (16 - 16 * u), b - 1)
                    hid_T(1 - u, b - 1)
                    x_T(1 - u, b + 1, 16 * j + 16)
                    down(1 - u, b - 1, 16 * j)
            last = 2 * n_pairs - 1
            gate_up(1, last, 16 * n_pairs, last - 1)
            for u in range(2):
                hid_T(u, last - 1 + u)
                down(u, last - 1 + u, 16 * n_pairs)

        @block.scalar
        def _(act):
            squares = [0]

            def square_sum(dst, src, junk=junk):
                if squares[0]:
                    act.wait_ge(squared, squares[0])
                squares[0] += 1
                act.activation(junk[:, 0:src.shape[-1]], src, ACT.Square, accum_out=dst).then_inc(squared, 1)

            def roots(dst, src, n):
                act.wait_ge(squared, squares[0])
                return act.activation(dst, src, ACT.Sqrt, bias=eps, scale=1.0 / n)

            act.wait_ge(vec_in, 48)
            act.activation(csil, vt[:, V_C:V_C + 8], ACT.Silu).then_inc(csil_ok, 1)
            for t in range(T):
                act.wait_ge(x_in[t // 4], 16)
                square_sum(xss[:, t:t + 1], xs[:, t, :], junk_x)
            act.wait_ge(const_in, 16)
            roots(xrt, xss, D).then_inc(x_root, 1)
            act.wait_ge(cols_ok, 1)
            for g in range(16):
                act.wait_ge(xT_mm, g + 1)
                if g >= 2:
                    act.wait_ge(h_split, g - 1)
                k = g % 8
                act.activation(hf[g % 2][:, :], ps[:, 2 + g % 4, :], ACT.Identity, bias=col_shift[:, k:k + 1],
                               scale=col_scale[:, k:k + 1]).then_inc(xT_f, 1)

            def win_round(n):
                act.wait_ge(win_in[n % 2], 16 * (n // 2) + 16)
                if n >= 2:
                    act.wait_ge(proj_mm, 8 * (n - 1) if n <= 6 else 40 + 4 * (n - 6))
                elif n == 0:
                    act.wait_ge(ada_acc, 8)
                act.activation(wh[n % 2][:, :, :], wf[n % 2][:, :, :], ACT.Copy).then_inc(win_hi, 1)

            win_round(0)
            for n in range(N_IN):
                if n + 1 < N_IN:
                    win_round(n + 1)
                if n == 3:
                    act.wait_ge(proj_out, 24)
                    act.wait_ge(bias_saved, 16 * 20)
                if n in (3, 4):
                    for t in range(T):
                        act.wait_ge(proj_mm, 8 * n + t + 1)
                        act.copy(vna[:, t, CH * (n - 3):CH * (n - 3) + CH], ps[:, t % 4, 0:CH]).then_inc(proj_out, 1)
                if n == 4:
                    for g in range(12):
                        act.wait_ge(swT_mm, g + 1)
                        dst = qall[:, g // 2, :] if g < 8 else kall[:, g // 2 - 4, :]
                        act.copy(dst[:, 512 * (g % 2):512 * (g % 2) + 512], ps[:, 4 + g % 4, :]).then_inc(swT_ev, 1)
                if n >= 5:
                    for g in range(4):
                        act.wait_ge(proj_mm, 41 + 4 * (n - 5) + g)
                        pair = 2 * ((n - 5) % 2) + g // 2
                        dst = qall[:, 4 + pair, :] if n < 7 else kall[:, 2 + pair, :]
                        act.copy(dst[:, 512 * (g % 2):512 * (g % 2) + 512], ps[:, g, :]).then_inc(proj_out, 1)

            def square_half(hp, i, done):
                act.wait_ge(squared, 2 * hp + (done + i))
                src = ot[:, ds(2 * hp + i, 1), 512:1024].rearrange("p a n -> p (a n)")
                act.activation(junk[:, 0:512], src, ACT.Square,
                               accum_out=oss[:, ds(2 * hp + (8 + i), 1)]).then_inc(squared, 1)

            def pt_copy(m, u0, window, slides):
                w = window(m // 2)[1]
                act.wait_ge(pT_mm, u0 + (m + 1))
                if m >= 2 or not isinstance(u0, int) or u0 > 0:
                    act.wait_ge(pv_mm, u0 + (m - 1))
                n4 = P * -(-min(w, 512) // P)
                last = act.copy(pt[m % 2][:, 0:n4], ps[:, T_bank(m, n4 // P), 0:n4])
                if w > 512:
                    last.then_inc(pt_half, 1)
                    last = act.copy(pt[m % 2][0:64, 512:640], ps[0:64, 5, 0:P])
                last.then_inc(pt_ok, 1)

            def attention(u0, window, slides, before, between=None):
                for n in range(16):
                    if between and n in (5, 12):
                        if n == 5:
                            act.wait_ge(o_ok, 64)
                        between(n // 12)
                    w = window(n // 2)[1]
                    act.wait_ge(logits_ok, u0 + (n + 1))
                    row = pb[n % 4][:, 0:w + slides]
                    act.activation(row, row, ACT.Exp, bias=asm[:, n:n + 1], scale=-1.0, accum_out=asm[:, 16 + n:17 + n]).then_inc(exp_ok, 1)
                    if n >= 1 and not on_dve(n - 1, slides):
                        pt_copy(n - 1, u0, window, slides)
                    elif n == 0 and before and not on_dve(15, before[1]):
                        pt_copy(15, u0 - 16, *before)

            attention(0, sw_win, True, None)
            with act.Fori(1, 4) as hp:
                attention(16 * hp, sw_win, True, (sw_win, True))
            done = squares[0]
            attention(64, na_win, False, (sw_win, True), lambda i: square_half(0, i, done))
            with act.Fori(1, 4) as hp:
                attention(16 * hp + 64, na_win, False, (na_win, False), lambda i: square_half(hp, i, done))
            squares[0] = done + T
            act.wait_ge(o_ok, 128)
            for t in range(T):
                square_sum(oss[:, t:t + 1], ot[:, t, 0:512])
                roots(ort.rearrange("p (g t) -> p g t", g=2)[:, :, t], oss.rearrange("p (g t) -> p g t", g=2)[:, :, t], 512).then_inc(o_root, 1)

            def mix_round(t):
                act.wait_ge(oT_mm, t + 1)
                if t >= 2:
                    act.wait_ge(mix_mm, t - 1)
                act.activation(mh[t % 2][:, :, :].rearrange("p k n -> p (k n)"), banks(0), ACT.Copy).then_inc(m_hi, 1)

            mix_round(0)
            for t in range(T):
                if t + 1 < T:
                    mix_round(t + 1)
                act.wait_ge(mix_mm, t + 1)
                square_sum(mst[:, t:t + 1], banks(2))
                roots(mst[:, 8 + t:9 + t], mst[:, t:t + 1], D).then_inc(mix_root, 1)
                act.wait_ge(x1_ok, t + 1)
                square_sum(gst[:, t:t + 1], x1[:, t, :])
                roots(gst[:, 8 + t:9 + t], gst[:, t:t + 1], D).then_inc(x1_root, 1)
                if t >= 1:
                    act.wait_ge(h2T_mm, t)
                    if t >= 2:
                        act.wait_ge(lg_mm, t - 1)
                    act.copy(h2T[:, :, :].rearrange("p k n -> p (k n)"), banks(4)).then_inc(h2T_ok, 1)
            act.wait_ge(h2T_mm, T)
            act.wait_ge(lg_mm, T - 1)
            act.copy(h2T[:, :, :].rearrange("p k n -> p (k n)"), banks(4)).then_inc(h2T_ok, 1)
            act.wait_ge(r_exp_in, 1)
            act.activation(rw[:, R_EX:R_EX + 40], rw[:, R_EI:R_EI + 40], ACT.Exp).then_inc(r_exp, 1)

            act.wait_ge(np_ok, 1)
            n_pairs = act.value_load(btab[0:1, MAXB:MAXB + 1], min_val=NE // 2 - 2, max_val=MAXB // 2 - 2) + 2

            def x_T(u, b):
                act.wait_ge(xgT_mm, b + 1)
                act.wait_ge(gu_mm, b - 1 if not isinstance(b, int) or b > 1 else 0)
                act.copy(xgT[u][:, 4:8, :].rearrange("p k n -> p (k n)"), ps[:, 3, :]).then_inc(xgT_b, 1)

            def silu(u, b):
                act.wait_ge(gu_mm, b + 1)
                act.activation(sg[u][:, :], ps[:, u, 0:FF], ACT.Silu).then_inc(sg_ok, 1)

            def gated(u, b, stored):
                act.wait_ge(dn_mm, b + 1)
                act.wait_ge(y_put[u], stored)
                act.activation(yg[u][:, 0:512], ps[:, 5, :], ACT.Copy, scale=tab[:, ds(b, 1), 2:3].bitcast(F32).rearrange("p a c -> p (a c)")).then_inc(yg_a, 1)

            act.wait_ge(tab_in, 16)
            x_T(0, 0)
            silu(0, 0)
            x_T(1, 1)
            with act.Fori(1, n_pairs) as j:
                for u in (1, 0):
                    b = 2 * j - u
                    silu(u, b)
                    x_T(1 - u, b + 1)
                    gated(1 - u, b - 1, 16 * j - 16)
            last = 2 * n_pairs - 1
            silu(1, last)
            gated(0, last - 1, 16 * n_pairs - 16)
            gated(1, last, 16 * n_pairs - 16)
            for t in range(T):
                act.wait_ge(y_sum, t + 1)
                square_sum(fst[:, t:t + 1], ya[t % 2][:, :])
                roots(fst[:, 8 + t:9 + t], fst[:, t:t + 1], D).then_inc(y_root, 1)

        @block.vector
        def _(dve):
            chain = [0, 0]

            def link(ins):
                chain[0] += 1
                ins.then_inc(dve_chain, 1)
                dve.wait_ge(dve_chain, chain[1] + chain[0])

            def looped(i, per, before):
                chain[0], chain[1] = before, per * i

            def weigh(acc, w, k):
                if k == 0:
                    link(dve.tensor_scalar(acc, w[:, 0, :], csil[:, 0:1], None, ALU.mult))
                else:
                    link(dve.scalar_tensor_tensor(acc, w[:, k, :], csil[:, k:k + 1], acc, ALU.mult, ALU.add))

            dve.wait_ge(const_in, 16)
            dve.wait_ge(vec_in, 48)
            link(dve.tensor_scalar(nsink[:, :], nsink[:, :], -1.0, None, ALU.mult))
            for g in range(16):
                dve.wait_ge(bias_mm, g + 1)
                table = bias_b[:, 0:14, :, 4 * g:4 * g + 4].rearrange("p m h c -> p (m h) c")
                src = ps[:, g % 2, 0:448].rearrange("p (c m) -> p m c", c=4)
                mask = bc(kt[:, C_NAM + 4 * g:C_NAM + 4 * g + 4].unsqueeze(1), 1, 112)
                dve.scalar_tensor_tensor(table, src, float(HD) ** 0.5, mask, ALU.mult, ALU.add).then_inc(bias_ev, 1)
            dve.wait_ge(bias_ev, 16)
            flat = bias_b[:, :, :, :].rearrange("p m h c -> p m (h c)")
            dve.tensor_scalar(flat[:, 14, :], flat[:, 2, :], kt[:, C_RQ1:C_RQ1 + 1], None, ALU.add)
            dve.tensor_scalar(flat[:, 15, :], flat[:, 10, :], kt[:, C_RQ0:C_RQ0 + 1], None, ALU.add).then_inc(bias_spec, 1)
            dve.wait_ge(csil_ok, 1)
            for c in range(4):
                dve.wait_ge(ada_in[c], 16)
                for k in range(K):
                    weigh(acc_a[:, c, :], adaA[c], k)
                dve.sem_inc(ada_acc, 1)
            dve.wait_ge(x_root, 1)
            link(dve.reciprocal(xrs, xrt))
            for t in range(T):
                dve.tensor_scalar(xs[:, t, :], xs[:, t, :], xrs[:, t:t + 1], None, ALU.mult).then_inc(x_scaled, 1)
            for c in range(4, 8):
                dve.wait_ge(ada_in[c - 4], 32)
                for k in range(K):
                    weigh(acc_a[:, c, :], adaA[c - 4], k)
                dve.sem_inc(ada_acc, 1)
            dve.wait_ge(modcol_mm, 1)
            link(dve.tensor_tensor(mcol, ps[:, 7, 0:16], vt[:, V_BADA:V_BADA + 16], ALU.add))
            dve.tensor_copy(col_shift, mcol[:, 0:8])
            link(dve.scalar_tensor_tensor(col_scale, mcol[:, 8:16], 1.0, vt[:, V_G:V_G + 8], ALU.add, ALU.mult))
            dve.sem_inc(cols_ok, 1)

            def win_rest(n):
                dve.wait_ge(win_hi, n + 1)
                dve.tensor_tensor(wl[n % 2][:, :, :], wf[n % 2][:, :, :], wh[n % 2][:, :, :].bitcast(F32), ALU.subtract).then_inc(win_lo, 1)

            for g in range(16):
                k, cols = g % 8, slice(512 * (g // 8), 512 * (g // 8) + 512)
                dve.wait_ge(xT_f, g + 1)
                link(dve.tensor_copy(hh[:, k, cols], hf[g % 2][:, :]))
                dve.tensor_tensor(hl[:, k, cols], hf[g % 2][:, :], hh[:, k, cols].bitcast(F32), ALU.subtract).then_inc(h_split, 1)

            def rope(src, heads, t, dst):
                cos = bc(kt[:, ds(C_COS + 64 * t, 64)].unsqueeze(1), 1, heads)
                sin = bc(kt[:, ds(C_SIN + 64 * t, 64)].unsqueeze(1), 1, heads)
                n = heads * HD
                a, b = (r[:, 0:n].rearrange("p (h c) -> p h c", c=HD) for r in (rt1, rt2))
                dve.tensor_tensor(a, src, cos, ALU.mult)
                dve.tensor_tensor(b[:, :, 0:32], src[:, :, 32:64], sin[:, :, 0:32], ALU.mult)
                link(dve.tensor_tensor(b[:, :, 32:64], src[:, :, 0:32], sin[:, :, 32:64], ALU.mult))
                if heads == 2:
                    for r in range(2):
                        last = dve.tensor_tensor(dst[:, :, r, :], a, b, ALU.add)
                    return last
                return dve.tensor_tensor(dst, a, b, ALU.add)

            win_rest(0)
            dve.wait_ge(bias_saved, 16 * 20)
            for n in range(3):
                win_rest(n + 1)
                before = chain[0]
                with dve.Fori(0, 2) as i:
                    looped(i, 8 if n == 0 else 4, before)
                    for q in range(4):
                        t = 4 * i + q
                        dve.wait_ge(proj_mm, 4 * i + (8 * n + q + 1))
                        dve.wait_ge(proj_out, 4 * i + (8 * n + q))
                        if n == 0:
                            link(dve.tensor_copy(svt[:, ds(t, 1), :].rearrange("p a n -> p (a n)"), ps[:, q, P:2 * P]))
                            dst = tmk[:, ds(t, 1), :].rearrange("p a (h r c) -> p (a h) r c", h=2, r=2)
                            rope(ps[:, q, 0:P].rearrange("p (h c) -> p h c", c=HD), 2, t, dst).then_inc(proj_out, 1)
                        else:
                            dst = tmq[:, ds(t, 1), CH * (n - 1):CH * n].rearrange("p a (h c) -> p (a h) c", c=HD)
                            rope(ps[:, q, 0:CH].rearrange("p (h c) -> p h c", c=HD), 4, t, dst).then_inc(proj_out, 1)
                per = chain[0] - before
                chain[0], chain[1] = before + 2 * per, 0
            for n in range(4, N_IN):
                win_rest(n)

            def scale_out(m, u0, hp, window, slides):
                a, j = m // 2, m % 2
                dve.wait_ge(exp_ok, u0 + (m + 1))
                total = asm[:, 16 + m:17 + m]
                link(dve.reciprocal(asm[:, 48 + m:49 + m], total))
                dve.wait_ge(pv_mm, u0 + (m + 1))
                col = (512 if slides else 0) + HD * j
                dve.tensor_scalar(ot[:, a, ds(P * hp + col, HD)], ps[:, 6 + j, 0:HD], asm[:, 48 + m:49 + m], None, ALU.mult).then_inc(o_ok, 1)

            def pt_copy(m, u0, window):
                w = window(m // 2)[1]
                dve.wait_ge(pT_mm, u0 + (m + 1))
                dve.wait_ge(pv_mm, u0 + (m - 1))
                n4 = P * -(-min(w, 512) // P)
                last = dve.tensor_copy(pt[m % 2][:, 0:n4], ps[:, T_bank(m, n4 // P), 0:n4])
                if w > 512:
                    last.then_inc(pt_half, 1)
                    last = dve.tensor_copy(pt[m % 2][0:64, 512:640], ps[0:64, 5, 0:P])
                last.then_inc(pt_ok, 1)

            def bias_of(a, j):
                _, n, s = na_window(a)
                return bias[:, s:s + n, HD * j:HD * j + HD]

            def mask_of(b, j):
                _, n, s = sw_window(b)
                return kt[:, C_SWM + P * s:C_SWM + P * (s + n)]

            def mod_row(pair, hp, window, slides):
                dve.wait_ge(rows_in, 48)
                dve.wait_ge(mod_mm, pair + 1)
                half = mods[:, :, :].rearrange("p r n -> p (r n)")[:, ds(512 * pair, 512)]
                plus = 0.0 if slides else kt[:, ds(C_PLUS + hp, 1)]
                dve.scalar_tensor_tensor(half, mod_bank(window), plus, half, ALU.add, ALU.mult).then_inc(mod_ok, 1)

            def attention(pair, hp, window, slides, before):
                u0 = 16 * pair
                if slides:
                    link(dve.tensor_copy(asm[:, 64:66], nsink[:, ds(2 * hp, 2)]))
                for n in range(16):
                    a, j = n // 2, n % 2
                    w = window(a)[1]
                    if not slides and n in (0, 4, 12):
                        dve.wait_ge(bias_in[(0, 4, 12).index(n)], 16 * hp + 16)
                    dve.wait_ge(qk_mm, u0 + (n + 1))
                    if n >= 4 or before:
                        dve.wait_ge(pT_mm, u0 + (n - 3))
                    dve.sem_inc(logits_due, 1)
                    if slides:
                        dve.tensor_copy(pb[n % 4][:, w:w + 1], asm[:, 64 + j:65 + j])
                    sh = (lambda ap: ap) if slides else (lambda ap: ap.rearrange("p (r c) -> p r c", c=GRID_W))
                    dve.tensor_tensor_reduce(sh(pb[n % 4][:, 0:w]), sh(banks(2 * j)[:, 0:w]), (mask_of if slides else bias_of)(a, j),
                                             -(float(HD) ** -0.5), asm[:, 64 + j:65 + j] if slides else 3.0e38, ALU.add, ALU.min,
                                             asm[:, n:n + 1]).then_inc(logits_ok, 1)
                    if n == 1 and before:
                        mod_row(pair - 1, *before)
                    if n >= 3:
                        scale_out(n - 3, u0, hp, window, slides)
                    elif before:
                        scale_out(n + 13, u0 - 16, *before)
                    if n >= 1 and on_dve(n - 1, slides):
                        pt_copy(n - 1, u0, window)
                    elif n == 0 and before and on_dve(15, before[2]):
                        pt_copy(15, u0 - 16, before[1])
                    if 2 <= n < 14:
                        for m in (2 * n - 4, 2 * n - 3) if n < 6 else (n + 2,):
                            c, k = m // K, m % K
                            if k == 0:
                                dve.wait_ge(adaC_in[c], 16 * pair + 16)
                            weigh(acc_c[:, c, :], adaC[c], k)
                        if n in (5, 13):
                            dve.sem_inc(adaC_used, 1)

            dve.wait_ge(proj_out, 56)
            dve.memset(mods[:, 1, :], 1.0)
            attention(0, 0, sw_win, True, None)
            before, per = chain[0], 16 + 1 + 16
            with dve.Fori(1, 4) as hp:
                looped(hp - 1, per, before)
                attention(hp, hp, sw_win, True, (hp - 1, sw_win, True))
                assert chain[0] - before == per, chain[0] - before
            chain[0], chain[1] = before + 3 * per, 0
            attention(4, 0, na_win, False, (3, sw_win, True))
            before, per = chain[0], 16 + 16
            with dve.Fori(1, 4) as hp:
                looped(hp - 1, per, before)
                attention(hp + 4, hp, na_win, False, (hp - 1, na_win, False))
                assert chain[0] - before == per, chain[0] - before
            chain[0], chain[1] = before + 3 * per, 0
            pt_copy(15, 112, na_win)
            for m in range(13, 16):
                scale_out(m, 112, 3, na_win, False)
            mod_row(7, 3, na_win, False)

            dve.wait_ge(beta_in, 16)

            def o_scale(t):
                if t >= 1:
                    dve.wait_ge(oT_mm, t)
                dve.wait_ge(o_root, t + 1)
                halves = lambda ap: ap.rearrange("p (g t) -> p g t", g=2)[:, :, t]
                link(dve.reciprocal(halves(ors), halves(ort)))
                for g in range(2):
                    cols = slice(512 * g, 512 * g + 512)
                    last = dve.scalar_tensor_tensor(osc[:, cols], ot[:, t, cols], ors[:, 8 * g + t:8 * g + t + 1], beta_b[:, cols], ALU.mult, ALU.mult)
                last.then_inc(os_ok, 1)

            def mix_rest(t):
                dve.wait_ge(m_hi, t + 1)
                dve.tensor_tensor(ml[t % 2][:, :, :].rearrange("p k n -> p (k n)"), banks(0),
                                  mh[t % 2][:, :, :].bitcast(F32).rearrange("p k n -> p (k n)"), ALU.subtract).then_inc(m_lo, 1)

            o_scale(0)
            mix_rest(0)
            o_scale(1)
            for t in range(T):
                if t + 1 < T:
                    mix_rest(t + 1)
                if t + 2 < T:
                    o_scale(t + 2)
                xt, ht, x1t = xb[t % 2][:, :], h2[t % 2][:, :], x1[:, t, :]
                dve.wait_ge(mix_root, t + 1)
                link(dve.reciprocal(mst[:, 16 + t:17 + t], mst[:, 8 + t:9 + t]))
                link(dve.scalar_tensor_tensor(x1t, banks(2), mst[:, 16 + t:17 + t], mods[:, 0, :], ALU.mult, ALU.mult))
                dve.wait_ge(xb_in[t % 2], 16 * (t // 2) + 16)
                dve.tensor_tensor(x1t, x1t, xt, ALU.add).then_inc(x1_ok, 1)
                if t >= 1:
                    dve.wait_ge(lg_mm, t - 1) if t >= 2 else None
                    if t >= 2:
                        dve.tensor_copy(lg[:, t - 2, :], ps[:, 6, 0:36]).then_inc(lg_ok, 1)
                dve.wait_ge(x1_root, t + 1)
                link(dve.reciprocal(gst[:, 16 + t:17 + t], gst[:, 8 + t:9 + t]))
                if t >= 2:
                    dve.wait_ge(h2_saved[t % 2], 16 * (t // 2))
                    dve.wait_ge(h2T_mm, t - 1)
                link(dve.scalar_tensor_tensor(ht, x1t, gst[:, 16 + t:17 + t], mods[:, 2, :], ALU.mult, ALU.mult))
                dve.tensor_tensor(ht, ht, mods[:, 1, :], ALU.add).then_inc(h2_ok, 1)
            for t in range(T - 2, T):
                dve.wait_ge(lg_mm, t + 1)
                dve.tensor_copy(lg[:, t, :], ps[:, 6, 0:36]).then_inc(lg_ok, 1)
            dve.wait_ge(lg_ok, T)

            def r(at, *dims):
                n = 1
                for d in dims:
                    n *= d
                ap = rw[:, at:at + n]
                if len(dims) == 2:
                    return ap.rearrange("p (a b) -> p a b", a=dims[0])
                if len(dims) == 3:
                    return ap.rearrange("p (a b c) -> p a b c", a=dims[0], b=dims[1])
                return ap

            def spread(ap, n):
                ap = ap.unsqueeze(len(ap.shape))
                return bc(ap, len(ap.shape) - 1, n)

            iota = kt[:, C_IOTA:C_IOTA + MAXB]
            link(dve.memset(r(R_G, 64), NEG))
            link(dve.tensor_copy(r(R_G, T, 8)[:, :, 0:NG], lg[:, :, 0:NG]))
            for t in range(T):
                last = dve.max(r(R_V, T, 8)[:, t, :], r(R_G, T, 8)[:, t, :])
            link(last)
            for t in range(T):
                last = dve.max_index(ru[:, 8 * t:8 * t + 8], r(R_V, T, 8)[:, t, :], r(R_G, T, 8)[:, t, :])
            link(last)
            link(dve.tensor_copy(r(R_GI, T), ru[:, 0:64].rearrange("p (t c) -> p t c", c=8)[:, :, 0]))
            link(dve.tensor_tensor(r(R_OG, T, NG), bc(iota[:, 0:NG].unsqueeze(1), 1, T), spread(r(R_GI, T), NG), ALU.is_equal))
            link(dve.tensor_tensor(r(R_EI, T, NG), lg[:, :, 0:NG], spread(r(R_V, T, 8)[:, :, 0], NG), ALU.subtract))
            link(dve.tensor_tensor(r(R_EM, T, NG, EPG), lg[:, :, NG:].rearrange("p t (g e) -> p t g e", g=NG), spread(r(R_OG, T, NG), EPG), ALU.mult))
            link(dve.tensor_scalar(r(R_OG, T * NG), r(R_OG, T * NG), -1.0, -NEG, ALU.add, ALU.mult))
            link(dve.tensor_tensor(r(R_EM, T, NG, EPG), r(R_EM, T, NG, EPG), spread(r(R_OG, T, NG), EPG), ALU.add))
            for t in range(T):
                last = dve.max(r(R_V, T, 8)[:, t, :], r(R_EM, T, NE)[:, t, :])
            link(last)
            for t in range(T):
                last = dve.max_index(ru[:, 8 * t:8 * t + 8], r(R_V, T, 8)[:, t, :], r(R_EM, T, NE)[:, t, :])
            link(last)
            for j in range(2):
                last = dve.tensor_copy(r(R_ID + T * j, T), ru[:, 0:64].rearrange("p (t c) -> p t c", c=8)[:, :, j])
            link(last)
            link(dve.tensor_tensor(r(R_EI + 32, T), r(R_V, T, 8)[:, :, 1], r(R_V, T, 8)[:, :, 0], ALU.subtract))
            dve.sem_inc(r_exp_in, 1)
            link(dve.tensor_tensor(r(R_O, 16, NE), bc(iota[:, 0:NE].unsqueeze(1), 1, 16), spread(r(R_ID, 16), NE), ALU.is_equal))
            link(dve.tensor_tensor(r(R_A, T, NE), r(R_O, T, NE), r(R_O + 256, T, NE), ALU.add))
            link(dve.memset(r(R_C, NE), 0.0))
            for t in range(T):
                link(dve.tensor_tensor(r(R_C + NE * (t + 1), NE), r(R_C + NE * t, NE), r(R_A + NE * t, NE), ALU.add))
            dve.sem_inc(r_pre, 1)
            dve.wait_ge(r_exp, 1)
            link(dve.tensor_reduce(r(R_GW, T), r(R_EX, T, NG), AX.X, ALU.add))
            link(dve.tensor_scalar(r(R_T, T), r(R_EX + 32, T), 1.0, None, ALU.add))
            link(dve.tensor_tensor(r(R_GW, T), r(R_GW, T), r(R_T, T), ALU.mult))
            link(dve.reciprocal(r(R_W, T), r(R_GW, T)))
            link(dve.tensor_tensor(r(R_W + T, T), r(R_W, T), r(R_EX + 32, T), ALU.mult))
            dve.wait_ge(pos_mm, 1)
            pos = r(R_M, 288)
            link(dve.tensor_copy(pos, ps[:, 7, 0:288]))
            for j in range(2):
                last = dve.tensor_tensor(r(R_T + 256 * j, 256), pos[:, 0:256], r(R_O + 256 * j, 256), ALU.mult)
            link(last)
            link(dve.tensor_reduce(r(R_P, 16), r(R_T, 16, NE), AX.X, ALU.add))
            step = kt[:, C_STEP:C_STEP + 7]
            link(dve.tensor_tensor(r(R_T, 16, 7), spread(r(R_P, 16), 7), bc(step.unsqueeze(1), 1, 16), ALU.is_ge))
            link(dve.tensor_reduce(r(R_B, 16), r(R_T, 16, 7), AX.X, ALU.add))
            link(dve.tensor_tensor(r(R_T, NE, 7), spread(pos[:, 256:288], 7), bc(step.unsqueeze(1), 1, NE), ALU.is_gt))
            link(dve.tensor_reduce(r(R_OB, NE), r(R_T, NE, 7), AX.X, ALU.add))
            link(dve.tensor_tensor_scan(r(R_OC, NE), r(R_OB, NE), r(R_OB, NE), 0.0, ALU.add, ALU.bypass))
            link(dve.tensor_tensor(r(R_OX, NE), r(R_OC, NE), r(R_OB, NE), ALU.subtract))
            link(dve.tensor_tensor(r(R_T, 16, NE), r(R_O, 16, NE), bc(r(R_OX, NE).unsqueeze(1), 1, 16), ALU.mult))
            link(dve.tensor_reduce(r(R_OS, 16), r(R_T, 16, NE), AX.X, ALU.add))
            link(dve.tensor_tensor(r(R_OS, 16), r(R_OS, 16), r(R_B, 16), ALU.add))
            link(dve.tensor_tensor(r(R_OS, 16), r(R_OS, 16), r(R_ID, 16), ALU.subtract))
            link(dve.tensor_scalar(r(R_OS, 16), r(R_OS, 16), float(NE - 1), None, ALU.add))
            link(dve.tensor_scalar(r(R_GE, 16), r(R_B, 16), 1.0, None, ALU.is_ge))
            link(dve.tensor_tensor(r(R_OS, 16), r(R_OS, 16), r(R_GE, 16), ALU.mult))
            link(dve.tensor_tensor(r(R_OS, 16), r(R_OS, 16), r(R_ID, 16), ALU.add))
            link(dve.scalar_tensor_tensor(r(R_OS, 16), r(R_P, 16), float(MAXB), r(R_OS, 16), ALU.mult, ALU.add))
            link(dve.scalar_tensor_tensor(r(R_OS, 16), r(R_B, 16), -float(MAXB * P), r(R_OS, 16), ALU.mult, ALU.add))
            dve.tensor_copy(ridx[:, :], r(R_OS, 16))
            tok = kt[:, C_TOK:C_TOK + 16]
            for j in range(2):
                dve.tensor_copy(rec[:, 8 * j:8 * j + 8, 0], tok[:, 0:8])
            dve.tensor_copy(rec[:, :, 1], tok)
            dve.tensor_copy(rec[:, :, 3], tok)
            link(dve.tensor_copy(rec[:, :, 2].bitcast(F32), r(R_W, 16)))
            dve.sem_inc(rec_ok, 1)
            extra = MAXB - NE
            link(dve.tensor_tensor(r(R_T, extra, NE), spread(iota[:, 0:extra], NE), bc(r(R_OC, NE).unsqueeze(1), 1, extra), ALU.is_ge))
            link(dve.tensor_reduce(r(R_BT + NE, extra), r(R_T, extra, NE), AX.X, ALU.add))
            link(dve.tensor_scalar(r(R_BT + NE, extra), r(R_BT + NE, extra), float(NE - 1), None, ALU.min))
            link(dve.tensor_copy(r(R_BT, NE), iota[:, 0:NE]))
            link(dve.tensor_tensor(r(R_T, 8), bc(r(R_OC + NE - 1, 1), 1, 8), kt[:, C_ODD:C_ODD + 8], ALU.is_ge))
            link(dve.tensor_reduce(r(R_BT + MAXB, 1), r(R_T, 8), AX.X, ALU.add))
            link(dve.tensor_scalar(r(R_BT + MAXB, 1), r(R_BT + MAXB, 1), float(NE // 2 - 2), None, ALU.add))
            link(dve.tensor_copy(btab[:, 0:MAXB + 1], r(R_BT, MAXB + 1)))
            dve.sem_inc(np_ok, 1)

            n_pairs = dve.value_load(btab[0:1, MAXB:MAXB + 1], min_val=NE // 2 - 2, max_val=MAXB // 2 - 2) + 2

            def x_T(u, b):
                dve.wait_ge(xgT_mm, b + 1)
                dve.wait_ge(gu_mm, b - 1 if not isinstance(b, int) or b > 1 else 0)
                dve.tensor_copy(xgT[u][:, 0:4, :].rearrange("p k n -> p (k n)"), ps[:, 2, :]).then_inc(xgT_a, 1)

            def hidden(u, b):
                dve.wait_ge(sg_ok, b + 1)
                dve.wait_ge(hidT_mm, b - 1 if not isinstance(b, int) or b > 1 else 0)
                dve.tensor_tensor(hid[u][:, :], ps[:, u, FF:2 * FF], sg[u][:, :], ALU.mult).then_inc(hid_ok, 1)

            def hid_T(u, b, used):
                dve.wait_ge(hidT_mm, b + 1)
                dve.wait_ge(dn_mm, used)
                dve.tensor_copy(hidT[u][:, :, :].rearrange("p k n -> p (k n)"), ps[:, 4, 0:FF]).then_inc(hidT_ok, 1)

            def gated(u, b, stored):
                dve.wait_ge(dn_mm, b + 1)
                dve.wait_ge(y_put[u], stored)
                dve.tensor_scalar(yg[u][:, 512:D], ps[:, 6, :], tab[:, ds(b, 1), 2:3].bitcast(F32).rearrange("p a c -> p (a c)"), None, ALU.mult).then_inc(yg_b, 1)

            for i in range(2):
                dve.wait_ge(h2_saved[i], 64)
            dve.wait_ge(tab_in, 16)
            x_T(0, 0)
            hidden(0, 0)
            x_T(1, 1)
            with dve.Fori(1, n_pairs) as j:
                for u in (1, 0):
                    b = 2 * j - u
                    hid_T(1 - u, b - 1, 2 * j - 2)
                    x_T(1 - u, b + 1)
                    hidden(u, b)
                    gated(1 - u, b - 1, 16 * j - 16)
            last = 2 * n_pairs - 1
            hid_T(0, last - 1, last - 1)
            hidden(1, last)
            gated(0, last - 1, 16 * n_pairs - 16)
            hid_T(1, last, last - 1)
            gated(1, last, 16 * n_pairs - 16)

            for t in range(T):
                y, o = ya[t % 2][:, :], yo[t % 2][:, :]
                dve.wait_ge(ya_in[t % 2], 16 * (t // 2) + 16)
                dve.wait_ge(yb_in[t % 2], 16 * (t // 2) + 16)
                dve.tensor_tensor(y, y, yb[t % 2][:, :], ALU.add).then_inc(y_sum, 1)
                dve.wait_ge(y_root, t + 1)
                link(dve.reciprocal(fst[:, 16 + t:17 + t], fst[:, 8 + t:9 + t]))
                if t >= 2:
                    dve.wait_ge(out_put[t % 2], 16 * (t // 2))
                link(dve.scalar_tensor_tensor(o, y, fst[:, 16 + t:17 + t], mods[:, 3, :], ALU.mult, ALU.mult))
                dve.tensor_tensor(o, o, x1[:, t, :], ALU.add).then_inc(yo_ok, 1)

        @block.gpsimd
        def _(pool):
            def stage(kind, t, q_at, k_at):
                cols = slice(P * t, P * t + P)
                if kind == "k":
                    dst, src = ks[:, cols], kall[:, k_at, cols]
                else:
                    dst, src = qz[:, kind, cols], qall[:, q_at, cols]
                src = src.rearrange("p a n -> p (a n)") if len(src.shape) == 3 else src
                if kind == "k":
                    pool.tensor_copy(dst, src).then_inc(staged, 1)
                else:
                    pool.tensor_tensor(dst, src, bc(kt[:, C_HEAD + kind:C_HEAD + kind + 1], 1, P), ALU.mult).then_inc(staged, 1)

            pool.wait_ge(swT_ev, 12)
            pool.wait_ge(win_lo, 9)
            for kind, t, _ in STAGE_SW:
                stage(kind, t, 0, 0)
            with pool.Fori(0, 4) as hp:
                for kind, t, a in STAGE_SW:
                    pool.wait_ge(qk_mm, 16 * hp + (2 * a + 2))
                    pool.sem_inc(stage_due, 1)
                    stage(kind, t, ds(hp + 1, 1), ds((hp + 1) // 2, 1))
            with pool.Fori(0, 3) as hp:
                for kind, t, a in STAGE_NA:
                    pool.wait_ge(qk_mm, 16 * hp + (64 + 2 * a + 2))
                    pool.sem_inc(stage_due, 1)
                    stage(kind, t, ds(hp + 5, 1), ds(hp + 3, 1))
            pool.wait_ge(staged, 8 * STEPS)
            for n in range(4):
                pool.wait_ge(wout_in[n], 16)
                pool.tensor_copy(woh[n][:, :, :], wof[n][:, :, :]).then_inc(wout_hi, 1)
                pool.wait_ge(wout_hi, n + 1)
                pool.tensor_tensor(wol[n][:, :, :], wof[n][:, :, :], woh[n][:, :, :].bitcast(F32), ALU.subtract).then_inc(wout_lo, 1)
            pool.memset(tab[:, :, :], BIG_ROW).then_inc(tab_fill, 1)
            pool.wait_ge(mix_mm, T)
            for i in range(2):
                pool.memset(xg[i][:, :], 0.0).then_inc(xg_zero, 1)
            pool.wait_ge(tab_init, 16)
            pool.wait_ge(rec_ok, 1)
            for i in range(16):
                pool.indirect_dma_start(tab_dram, bass.IndirectOffsetOnAxis(ap=ridx[:, i:i + 1], axis=0), rec[:, i, :], None,
                                        bounds_check=P * MAXB - 1, oob_is_err=False).then_inc(tab_put, 16)
            pool.wait_ge(np_ok, 1)
            n_pairs = pool.value_load(btab[0:1, MAXB:MAXB + 1], min_val=NE // 2 - 2, max_val=MAXB // 2 - 2) + 2
            pool.wait_ge(tab_in, 16)
            pool.wait_ge(xg_zero, 2)
            for i in range(2):
                pool.wait_ge(h2_saved[i], 64)

            def index_in(dst, b, col, count):
                pool.tensor_copy(dst[:, :], tab[:, ds(b, 1), col:col + 1].rearrange("p a c -> p (a c)")).then_inc(ix_ok, 1)
                pool.wait_ge(ix_ok, count)
                pool.sem_inc(ix_due, 1)

            def fetch(u):
                pool.indirect_dma_start(xg[u][:, :], None, h2_dram, bass.IndirectOffsetOnAxis(ap=ixg[u][:, 0:1], axis=0),
                                        bounds_check=S - 1, oob_is_err=False).then_inc(xg_in[u], 16)

            def store(u, b, count):
                pool.wait_ge(yg_a, b + 1)
                pool.wait_ge(yg_b, b + 1)
                index_in(ixs[u], b, 1, count)
                pool.indirect_dma_start(y2_dram, bass.IndirectOffsetOnAxis(ap=ixs[u][:, 0:1], axis=0), yg[u][:, :], None,
                                        bounds_check=2 * S - 1, oob_is_err=False).then_inc(y_put[u], 16)

            def gather(u, b, count):
                index_in(ixg[u], b, 0, count)
                fetch(u)

            for b in range(4):
                if b >= 2:
                    pool.wait_ge(xgT_mm, b - 1)
                    pool.wait_ge(xg_in[b % 2], 16)
                gather(b % 2, b, b + 1)
            with pool.Fori(1, n_pairs - 1) as j:
                for u in (1, 0):
                    b = 2 * j - u
                    pool.wait_ge(xgT_mm, b + 2)
                    pool.wait_ge(xg_in[1 - u], 16 * j + 16)
                    gather(1 - u, b + 3, 4 * j + (3 - 2 * u))
                    store(1 - u, b - 1, 4 * j + (4 - 2 * u))
            for i in range(4):
                store(i % 2, 2 * n_pairs - 4 + i, 4 * n_pairs - 3 + i)
            for u in range(2):
                pool.wait_ge(y_put[u], 16 * n_pairs)
            pool.sem_inc(moe_done, 1)


def constants():
    c = np.zeros((P, C_END), np.float32)
    c[:, C_ID:C_ID + P] = np.eye(P)
    c[:, C_ONE:C_ONE + P] = 1
    c[:, C_TRI:C_TRI + P] = np.triu(np.ones((P, P)), 1)
    inv = np.float32(10000.0) ** (-np.arange(HD // 2, dtype=np.float32) * np.float32(2.0) / np.float32(HD))
    ang = np.arange(S, dtype=np.float32)[:, None] * inv[None, :].astype(np.float32)
    cos, sin = np.cos(ang).astype(np.float32), np.sin(ang).astype(np.float32)
    lay = lambda a: a.reshape(T, P, HD).transpose(1, 0, 2).reshape(P, T * HD)
    c[:, C_COS:C_COS + T * HD] = lay(np.concatenate([cos, cos], 1))
    c[:, C_SIN:C_SIN + T * HD] = lay(np.concatenate([-sin, sin], 1))
    q, key = np.arange(P)[:, None], np.arange(3 * P)[None, :] - P
    c[:, C_SWM:C_SWM + 3 * P] = np.where(np.abs(key - q) <= P, 0, NEG)
    col, kc = (np.arange(P) % GRID_W)[:, None], np.arange(GRID_W)[None, :]
    start = np.clip(col - KW // 2, 0, GRID_W - KW)
    c[:, C_NAM:C_NAM + GRID_W] = np.where((kc >= start) & (kc < start + KW), 0, NEG)
    for r in range(2):
        for dc in range(2 * KW - 1):
            c[32 * r + dc, C_SEL + 64 * r + 78 - dc] = 1
    c[:, C_IOTA:C_IOTA + MAXB] = np.arange(MAXB)
    c[:, C_STEP:C_STEP + 8] = P * (1 + np.arange(8))
    c[:, C_ODD:C_ODD + 8] = 1 + 2 * np.arange(8)
    tok = np.arange(P)[:, None] + P * np.arange(T)[None, :]
    c[:, C_TOK:C_TOK + 16] = np.concatenate([tok, tok + S], 1)
    c[:, C_RQ0], c[:, C_RQ1] = np.where(np.arange(P) < 64, NEG, 0), np.where(np.arange(P) < 64, 0, NEG)
    c[:, C_EPS] = EPS
    c[:64, C_HEAD], c[64:, C_HEAD + 1] = 1, 1
    c[:, C_PLUS:C_PLUS + 2] = 1
    return c


def kernel(**a):
    import concourse.bacc as bacc
    from concourse.bass_utils import run_bass_kernel_spmd

    a = {k: np.asarray(v) for k, v in a.items()}
    cols = lambda v: v.reshape(-1, P).T

    def chunks(w, order):
        n = w.shape[1] // CH
        return np.ascontiguousarray(w.reshape(K, P, n, CH).transpose(2, 1, 0, 3)[order])

    b = a["b_ada"][0]
    rpb = a["na_rpb"][0]
    rcols = np.zeros((63, 14, 8), np.float32)
    for r in range(2):
        rcols[32 * r:32 * r + 31] = rpb[:, 1 - r:15 - r, :].transpose(2, 1, 0)
    wr = np.concatenate([a["w_group_router"][0]] + [a["w_expert_router"][0, g] for g in range(NG)], 1)
    gu = np.concatenate([a["w_gate"][0], a["w_up"][0]], 2)
    arrays = {
        "x": a["x"][0],
        "consts": constants(),
        "vecs": np.concatenate([cols(b[:2 * D]), cols(a["g_pre_mix"][0]), cols(a["beta_na"][0]), cols(a["beta_swa"][0]), cols(a["c"][0])], 1),
        "b_rows": b[2 * D:].reshape(8, 512),
        "g_rows": np.stack([a["g_post_mix"][0], a["g_pre_ffn"][0], a["g_post_ffn"][0],
                            np.concatenate([a["beta_na"][0], a["beta_swa"][0]])]),
        "rpb_cols": rcols.reshape(63, 112),
        "sinks": a["swa_sinks"],
        "w_ada": chunks(a["w_ada"][0], np.arange(24)),
        "w_in": chunks(a["w_in"][0], np.array([8, 6, 7, 4, 5, 0, 1, 2, 3])),
        "w_out": chunks(a["w_out"][0], np.arange(4)),
        "w_router": wr.reshape(K, P, 36).transpose(1, 0, 2),
        "w_gu": gu.reshape(NE, K, P, 2 * FF).transpose(0, 2, 1, 3),
        "w_down": a["w_down"][0].reshape(NE, 2, P, D).transpose(0, 2, 1, 3),
    }
    arrays = {f"in_{k}": np.ascontiguousarray(v) for k, v in arrays.items()}
    nc = bacc.Bacc("TRN2", target_bir_lowering=False, num_devices=1)
    aps = [nc.dram_tensor(k, v.shape, mybir.dt.from_np(v.dtype), kind="ExternalInput").ap() for k, v in arrays.items()]
    out = nc.dram_tensor("out_dram", (S, D), F32, kind="ExternalOutput").ap()
    build(nc, *aps, out)
    r = run_bass_kernel_spmd(nc, [arrays], core_ids=[0])
    return r.results[0]["out_dram"].reshape(1, S, D)
```

```python
import numpy as np

import concourse.bass as bass
from concourse import mybir
from concourse.alu_op_type import AluOpType as ALU
from contextlib import ExitStack

F32 = mybir.dt.float32
F32R = mybir.dt.float32r
BF16 = mybir.dt.bfloat16
U32 = mybir.dt.uint32
ACT = mybir.ActivationFunctionType
AX = mybir.AxisListType
ds = bass.ds

P = 128
S = 1024
T = S // P
D = 1024
K = D // P
GRID_W = 64
HD = 64
KH, KW = 8, 16
ROWS = S // GRID_W
NG, EPG = 4, 8
NE = NG * EPG
FF = 256
EPS = 1e-6
NEG = -1e30
CH = 256
N_IN = 9
SLICES = 29
BIAS_PARTS = ((0, 10), (10, 19), (19, 29))
MAXB = 48
MISS = float(4 * S)

C_ID, C_ONE, C_TRI, C_COS, C_SIN = 0, 128, 256, 384, 384 + 512
C_SWM = 384 + 1024
C_NAM = C_SWM + 384
C_SEL = C_NAM + 64
C_IOTA = C_SEL + 256
C_STEP = C_IOTA + 48
C_ODD = C_STEP + 8
C_TOK = C_ODD + 8
C_RQ0, C_RQ1, C_EPS = C_TOK + 16, C_TOK + 17, C_TOK + 18
C_PLUS = C_TOK + 19
C_HEAD = C_PLUS + 4
C_LANE = C_PLUS + 6
C_END = C_LANE + P

R_A, R_C, R_O = 0, 256, 544
R_EM, R_G, R_V, R_T = 1056, 1312, 1376, 1440
R_EI, R_EX = 2240, 2280
R_OG, R_GI, R_GW, R_W, R_ID, R_P, R_B, R_OS = (2320 + x for x in (0, 32, 40, 48, 64, 80, 96, 112))
R_OB, R_OC, R_OX, R_BT, R_END = 1056, 1088, 1120, 1152, 2464

V_BADA, V_G, V_C = 0, 16, 24
V_END = 32


def na_window(a):
    r0 = min(max(2 * a - KH // 2, 0), ROWS - KH)
    r1 = min(max(2 * a + 1 - KH // 2, 0), ROWS - KH)
    n = r1 + KH - r0
    if n == KH + 1:
        return r0, n, 10
    return r0, n, r0 - 2 * a + (2 if a < 2 else 25)


def bc(ap, axis, n):
    shape = list(ap.shape)
    shape[axis] = n
    return ap.broadcast_to(shape)


def sw_window(b):
    lo, hi = max(b - 1, 0), min(b + 1, T - 1)
    return lo, hi - lo + 1, lo - b + 1


def build(nc, x, consts, vecs, b_rows, g_rows, rpb_cols, sinks, w_mix_ada, w_ada, w_in, w_out, w_router, w_gu, w_down, out):
    BASE = 16512

    def sbt(name, shape, dt, kb):
        return nc.alloc_sbuf_tensor_at(name, shape, dt, offset=int(kb * 1024) + BASE)

    with ExitStack() as ctx:
        def sem(name):
            return ctx.enter_context(nc.semaphore(name))

        kt = sbt("kt", [P, C_END], F32, 0)
        vt = sbt("vt", [P, V_END], F32, 206.25)
        nsink = sbt("nsink", [P, 8], F32, 206.5)
        small = sbt("small", [P, 188], F32, 206.625)
        svt = sbt("svt", [P, T, P], F32, 202)
        vna = sbt("vna", [P, T, 512], F32, 10)
        rcol = sbt("rcol", [63, 112], F32, 22.0)
        junk_x = sbt("junk_x", [P, D], BF16, 22.5)
        junk = sbt("junk", [P, D], BF16, 198)
        acc_a = sbt("acc_a", [P, 4, 512], F32, 58)
        adaA = [sbt(f"adaA{i}", [P, K, 512], F32, (106, 122, 26, 42)[i]) for i in range(4)]
        xs = sbt("xs", [P, T, D], F32, 170)
        bias_b = sbt("bias_b", [P, 16, 8, 64], F32, 138)
        hf = [sbt(f"hf{i}", [P, 512], F32, 10 + 2 * i) for i in range(4)]
        hh = sbt("hh", [P, K, S], F32R, 26)
        hl = sbt("hl", [P, K, S], F32R, 58)
        wf = [sbt(f"wf{i}", [P, K, CH], F32, 90 + 8 * i) for i in range(2)]
        wh = [sbt(f"wh{i}", [P, K, CH], F32R, 106 + 16 * i) for i in range(2)]
        wl = [sbt(f"wl{i}", [P, K, CH], F32R, 114 + 16 * i) for i in range(2)]
        tmq = sbt("tmq", [P, T, 512], F32, 154)
        tmk = sbt("tmk", [P, T, 256], F32, 178)
        rt1 = sbt("rt1", [P, CH], F32, 22)
        rt2 = sbt("rt2", [P, CH], F32, 23)
        qall = sbt("qall", [P, 8, S], F32, 138)
        kall = sbt("kall", [P, 6, S], F32, 170)
        ot = sbt("ot", [P, T, D], F32, 26)
        adaC = [sbt(f"adaC{i}", [P, K, CH], F32, 58 + 8 * i) for i in range(2)]
        mods = sbt("mods", [P, 4, D], F32, 74)
        bias = sbt("bias", [P, SLICES, P], F32, 106)
        acc_c = sbt("acc_c", [P, 2, CH], F32, 90)
        b_row = sbt("b_row", [1, 512], F32, 92)
        beta_b = sbt("beta_b", [P, D], F32, 194)
        qz = sbt("qz", [P, 2, S], F32, 94)
        ks = sbt("ks", [P, S], F32, 102)
        pb = [sbt(f"pb{i}", [P, 576], F32, 122 + 2.25 * i) for i in range(4)]
        pt = [sbt(f"pt{i}", [P, 640], F32, 131 + 2.5 * i) for i in range(2)]
        asm = sbt("asm", [P, 128], F32, 136)
        WO = (138, 146, 170, 58)
        wof = [sbt(f"wof{i}", [P, K, CH], F32, WO[i]) for i in range(4)]
        wol = [sbt(f"wol{i}", [P, K, CH], F32R, WO[i]) for i in range(4)]
        woh = [sbt(f"woh{i}", [P, K, CH], F32R, (154, 162, 178, 186)[i]) for i in range(4)]
        mh = [sbt(f"mh{i}", [P, K, P], F32R, (106, 98)[i]) for i in range(2)]
        ml = [sbt(f"ml{i}", [P, K, P], F32R, (110, 102)[i]) for i in range(2)]
        osc = sbt("osc", [P, D], F32, 114)
        xb = [sbt(f"xb{i}", [P, D], F32, 118 + 4 * i) for i in range(2)]
        h2 = [sbt(f"h2{i}", [P, D], F32, 126 + 4 * i) for i in range(2)]
        h2T = sbt("h2T", [P, K, P], F32, 70)
        x1 = sbt("x1", [P, T, D], F32, 26)
        lg = sbt("lg", [P, T, 36], F32, 136.75)
        wrt = sbt("wrt", [P, K, 36], F32, 66)
        rw = sbt("rw", [P, 2560], F32, 90)
        lanes = sbt("lanes", [P, 16, P], F32, 106)
        recs = sbt("recs", [P, 16, 2 * MAXB], F32, 58)
        blocks = sbt("blocks", [P, 16, MAXB], F32, 114)
        btab = sbt("btab", [P, 64], U32, 100.75)
        ru = sbt("ru", [P, 128], U32, 101)
        tab = sbt("tab", [P, MAXB, 4], U32, 204)
        ixg = [sbt(f"ixg{i}", [P, 1], U32, 206 + 0.0625 * i) for i in range(2)]
        ixs = [sbt(f"ixs{i}", [P, 1], U32, 206.125 + 0.0625 * i) for i in range(2)]
        wgu = [sbt(f"wgu{i}", [P, K, 512], F32, 138 + 16 * i) for i in range(2)]
        wd = [sbt(f"wd{i}", [P, 2, D], F32, 170 + 8 * i) for i in range(2)]
        xg = [sbt(f"xg{i}", [P, D], F32, 106 + 4 * i) for i in range(2)]
        xgT = [sbt(f"xgT{i}", [P, K, P], F32, 114 + 4 * i) for i in range(2)]
        sg = [sbt(f"sg{i}", [P, FF], F32, 122 + i) for i in range(2)]
        hid = [sbt(f"hid{i}", [P, FF], F32, 124 + i) for i in range(2)]
        hidT = [sbt(f"hidT{i}", [P, 2, P], F32, 126 + i) for i in range(2)]
        yg = [sbt(f"yg{i}", [P, D], F32, 128 + 4 * i) for i in range(2)]
        yab = sbt("yab", [P, T, 2, D], F32, 138)
        ps = ctx.enter_context(nc.psum_tensor("ps", [P, 8, 512], F32))

        ident, ones, tri = kt[:, C_ID:C_ID + P], kt[:, C_ONE:C_ONE + P], kt[:, C_TRI:C_TRI + P]
        eps = kt[:, C_EPS:C_EPS + 1]
        col_scale, col_shift = small[:, 0:8], small[:, 8:16]
        xss, xrt, xrs = small[:, 16:24], small[:, 24:32], small[:, 32:40]
        oss, ort, ors = small[:, 40:56], small[:, 56:72], small[:, 72:88]
        csil = small[:, 88:96]
        mst, gst, fst = small[:, 96:120], small[:, 120:144], small[:, 144:168]
        mcol = small[:, 168:184]

        def banks(b, n=2):
            return ps[:, b:b + n, :].rearrange("p b n -> p (b n)")

        bias_dram = nc.dram_tensor("bias_dram", [4, P, SLICES, P], F32).ap()
        h2_dram = nc.dram_tensor("h2_dram", [S, D], F32).ap()
        y2_dram = nc.dram_tensor("y2_dram", [2 * S, D], F32).ap()

        const_in, vec_in, x_in = sem("const_in"), sem("vec_in"), [sem(f"x_in{i}") for i in range(2)]
        ada_in = [sem(f"ada_in{i}") for i in range(4)]
        ada_acc, csil_ok, bias_mm, bias_ev, bias_spec = sem("ada_acc"), sem("csil_ok"), sem("bias_mm"), sem("bias_ev"), sem("bias_spec")
        modcol_mm, cols_ok, bias_saved = sem("modcol_mm"), sem("cols_ok"), sem("bias_saved")
        squared, x_root, xr_ok, x_act, x_dve, x_pool, xT_mm, xT_f, h_high, h_split = (sem(n) for n in ("squared", "x_root", "xr_ok", "x_act", "x_dve", "x_pool", "xT_mm", "xT_f", "h_high", "h_split"))
        win_in, win_hi, win_lo = [sem(f"win_in{i}") for i in range(2)], sem("win_hi"), sem("win_lo")
        proj_mm, proj_out, swT_mm, swT_ev, dve_chain = (sem(n) for n in ("proj_mm", "proj_out", "swT_mm", "swT_ev", "dve_chain"))
        bias_in, adaC_in, rows_in, brow_in = [sem(f"bias_in{i}") for i in range(3)], [sem(f"adaC_in{i}") for i in range(2)], sem("rows_in"), sem("brow_in")
        stage_due = sem("stage_due")
        staged = sem("staged")
        qk_mm, logits_ok, exp_ok, pT_mm, pt_ok, pv_mm, o_ok = (
            sem(n) for n in ("qk_mm", "logits_ok", "exp_ok", "pT_mm", "pt_ok", "pv_mm", "o_ok"))
        adaC_used, mod_mm, mod_ok = (sem(n) for n in ("adaC_used", "mod_mm", "mod_ok"))
        o_root, logits_due, ix_due = sem("o_root"), sem("logits_due"), sem("ix_due")
        wout_in, beta_in, wout_hi, wout_lo, router_in = [sem(f"wout_in{i}") for i in range(4)], sem("beta_in"), sem("wout_hi"), sem("wout_lo"), sem("router_in")
        mix_out = sem("mix_out")
        os_ok, oT_mm, m_hi, m_lo, mix_mm, mix_root, x1_ok, x1_root = (
            sem(n) for n in ("os_ok", "oT_mm", "m_hi", "m_lo", "mix_mm", "mix_root", "x1_ok", "x1_root"))
        xb_in = [sem(f"xb_in{i}") for i in range(2)]
        h2_ok, h2_saved = sem("h2_ok"), [sem(f"h2_saved{i}") for i in range(2)]
        h2T_mm, h2T_ok, lg_mm, lg_ok = (sem(n) for n in ("h2T_mm", "h2T_ok", "lg_mm", "lg_ok"))
        r_exp, r_pre, pos_mm, r_exp_in, lane_ok = (sem(n) for n in ("r_exp", "r_pre", "pos_mm", "r_exp_in", "lane_ok"))
        rec_ok, tab_mm, tab_in, np_ok = (sem(n) for n in ("rec_ok", "tab_mm", "tab_in", "np_ok"))
        gu_in, dn_in = [sem(f"gu_in{i}") for i in range(2)], [sem(f"dn_in{i}") for i in range(2)]
        ix_ok, xg_in = sem("ix_ok"), [sem(f"xg_in{i}") for i in range(2)]
        xgT_mm, xgT_a, xgT_b, gu_mm, sg_ok, hid_ok, hidT_mm, hidT_ok, dn_mm, yg_a, yg_b = (
            sem(n) for n in ("xgT_mm", "xgT_a", "xgT_b", "gu_mm", "sg_ok", "hid_ok", "hidT_mm", "hidT_ok", "dn_mm", "yg_a", "yg_b"))
        y_put = [sem(f"y_put{i}") for i in range(2)]
        moe_done, y_in = sem("moe_done"), [sem(f"y_in{t}") for t in range(T)]
        y_sum, y_root, yo_ok = [sem(f"y_sum{i}") for i in range(2)], *(sem(n) for n in ("y_root", "yo_ok"))
        out_put = sem("out_put")

        def na_win(a):
            r0, n, _ = na_window(a)
            return GRID_W * r0, GRID_W * n

        def sw_win(b):
            lo, n, _ = sw_window(b)
            return P * lo, P * n

        def tiles(window, a):
            first, width = window(a)
            return range(first // P, -(-(first + width) // P))

        def staging(window):
            return [(kind, t, a) for a in range(T) for kind in (0, 1, "k") for t in range(T)
                    if a == (max(b for b in range(T) if t in tiles(window, b)) if kind == "k" else t)]

        def needed(window, orders, a):
            want = {(0, a), (1, a)} | {("k", t) for t in tiles(window, a)}
            return max(max(i for i, (kind, t, _) in enumerate(o) if (kind, t) in want) + 1 for o in orders)

        STAGE_SW, STAGE_NA = staging(sw_win), staging(na_win)
        STEPS = len(STAGE_SW)
        mod_bank = lambda window: ps[:, 1 if window is sw_win else 5, :]
        T_bank = lambda n, nb: 4 + (n % 2 if nb <= 3 else 0)
        on_dve = lambda n, slides: not slides and n % 4 == 3

        block = ctx.enter_context(nc.Block())

        @block.sync
        def _(sp):
            sp.dma_start(kt[:, :], consts).then_inc(const_in, 16)
            sp.dma_start(vt[:, :], vecs).then_inc(vec_in, 16)
            sp.dma_start(rcol[:, :], rpb_cols).then_inc(vec_in, 16)
            sp.dma_start(nsink[:, :], sinks[0:1, :].broadcast_to([P, 8])).then_inc(vec_in, 16)
            for i in range(2):
                for c in range(2 * i, 2 * i + 2):
                    sp.dma_start(adaA[c][:, :, :], w_mix_ada[c]).then_inc(ada_in[c], 16)
                sp.dma_start(xs[:, 4 * i:4 * i + 4, :],
                             x[512 * i:512 * i + 512, :].rearrange("(t p) d -> p t d", p=P)).then_inc(x_in[i], 16)
            for i in range(2):
                sp.dma_start(wf[i][:, :, :], w_in[i]).then_inc(win_in[i], 16)
            sp.wait_ge(bias_spec, 2)
            for hp in range(4):
                pair = bias_b[:, :, 2 * hp:2 * hp + 2, :].rearrange("p m h c -> p m (h c)")
                for dst, src, n in ((0, 4, 10), (10, 14, 1), (11, 3, 7), (18, 15, 1), (19, 0, 10)):
                    sp.dma_start(bias_dram[hp, :, dst:dst + n, :], pair[:, src:src + n, :]).then_inc(bias_saved, 16)
            for n in range(2, N_IN):
                sp.wait_ge(win_hi, n - 1)
                sp.wait_ge(win_lo, n - 1)
                sp.dma_start(wf[n % 2][:, :, :], w_in[n]).then_inc(win_in[n % 2], 16)
            sp.wait_ge(bias_saved, 16 * 20)
            sp.wait_ge(proj_mm, 56)
            for i in range(2):
                sp.dma_start(adaC[i][:, :, :], w_ada[i]).then_inc(adaC_in[i], 16)
            sp.dma_start(b_row[:, :], b_rows[0:1, :]).then_inc(brow_in, 16)
            for i in range(3):
                sp.dma_start(mods[:, (0, 2, 3)[i], :], g_rows[i:i + 1, :].broadcast_to([P, D])).then_inc(rows_in, 16)
            for i, (s0, s1) in enumerate(BIAS_PARTS):
                sp.dma_start(bias[:, s0:s1, :], bias_dram[0, :, s0:s1, :]).then_inc(bias_in[i], 16)
            sp.dma_start(beta_b[:, :], g_rows[3:4, :].broadcast_to([P, D])).then_inc(beta_in, 16)

            def next_ada(i, pair):
                sp.wait_ge(adaC_used, 2 * pair + (i + 1))
                sp.dma_start(adaC[i][:, :, :], w_ada[ds(2 * pair + (2 + i), 1)].rearrange("a p k n -> (a p) k n")).then_inc(adaC_in[i], 16)

            def next_b(pair):
                sp.wait_ge(mod_mm, pair + 1)
                sp.dma_start(b_row[:, :], b_rows[ds(pair + 1, 1), :]).then_inc(brow_in, 16)

            def next_bias(i, hp, tile):
                s0, s1 = BIAS_PARTS[i]
                sp.wait_ge(logits_ok, 16 * hp + (64 + 2 * tile + 2))
                sp.dma_start(bias[:, s0:s1, :], bias_dram[ds(hp + 1, 1), :, s0:s1, :].rearrange("a p s n -> (a p) s n")).then_inc(bias_in[i], 16)

            with sp.Fori(0, 4) as hp:
                next_ada(0, hp)
                next_ada(1, hp)
                next_b(hp)
            sp.wait_ge(staged, 5 * STEPS)
            for n in range(3):
                sp.dma_start(wof[n][:, :, :], w_out[n]).then_inc(wout_in[n], 16)
            with sp.Fori(0, 3) as hp:
                next_bias(0, hp, 1)
                next_ada(0, hp + 4)
                next_bias(1, hp, 5)
                next_ada(1, hp + 4)
                next_b(hp + 4)
                next_bias(2, hp, 7)
            sp.wait_ge(adaC_used, 15)
            sp.dma_start(wof[3][:, :, :], w_out[3]).then_inc(wout_in[3], 16)
            sp.wait_ge(adaC_used, 16)
            sp.dma_start(wrt[:, :, :], w_router).then_inc(router_in, 16)
            for t in range(T):
                if t == 0:
                    sp.wait_ge(pv_mm, 128)
                if t >= 2:
                    sp.wait_ge(x1_ok, t - 1)
                sp.dma_start(xb[t % 2][:, :], x[P * t:P * t + P, :]).then_inc(xb_in[t % 2], 16)
                if t >= 1:
                    sp.wait_ge(h2_ok, t)
                    sp.dma_start(h2_dram[P * t - P:P * t, :], h2[(t - 1) % 2][:, :]).then_inc(h2_saved[(t - 1) % 2], 16)
            sp.wait_ge(h2_ok, T)
            sp.dma_start(h2_dram[P * T - P:P * T, :], h2[(T - 1) % 2][:, :]).then_inc(h2_saved[(T - 1) % 2], 16)
            sp.wait_ge(mix_mm, T)
            for i in range(2):
                sp.dma_start(wgu[i][:, :, :], w_gu[i]).then_inc(gu_in[i], 16)
                sp.dma_start(wd[i][:, :, :], w_down[i]).then_inc(dn_in[i], 16)
            sp.wait_ge(np_ok, 1)
            n_pairs = sp.value_load(btab[0:1, MAXB:MAXB + 1], min_val=NE // 2 - 2, max_val=MAXB // 2 - 2) + 2

            def expert(b):
                return sp.value_load(btab[0:1, ds(b, 1)], min_val=0, max_val=NE - 1)

            def load_gu(u, b):
                e = expert(b)
                sp.wait_ge(gu_mm, b - 1)
                sp.dma_start(wgu[u][:, :, :], w_gu[ds(e, 1)].rearrange("a p k n -> (a p) k n")).then_inc(gu_in[u], 16)

            def load_dn(u, b):
                e = expert(b)
                sp.wait_ge(dn_mm, b - 1)
                sp.dma_start(wd[u][:, :, :], w_down[ds(e, 1)].rearrange("a p k n -> (a p) k n")).then_inc(dn_in[u], 16)

            load_gu(0, 2)
            with sp.Fori(1, n_pairs - 1) as j:
                for u in range(2):
                    load_gu(1 - u, 2 * j + (u + 1))
                    load_dn(u, 2 * j + u)
            load_gu(1, 2 * n_pairs - 1)
            for u in range(2):
                load_dn(u, 2 * n_pairs - 2 + u)
            sp.wait_ge(moe_done, 1)
            both = y2_dram.rearrange("(c t p) d -> t p c d", c=2, p=P)
            for t in range(T):
                sp.dma_start(yab[:, t, :, :], both[t]).then_inc(y_in[t], 16)
            for t in range(T):
                sp.wait_ge(yo_ok, t + 1)
                sp.dma_start(out[P * t:P * t + P, :], yab[:, t, 1, :]).then_inc(out_put, 16)
            sp.wait_ge(out_put, 16 * T)

        @block.tensor
        def _(pe):
            def three(dst, ah, al, bh, bl, first, last):
                pe.matmul(dst, ah, bh, start=first, stop=False)
                pe.matmul(dst, al, bh, start=False, stop=False)
                return pe.matmul(dst, ah, bl, start=False, stop=last)

            pe.wait_ge(const_in, 16)
            pe.wait_ge(vec_in, 48)
            def bias_products(groups):
                for g in groups:
                    if g >= 4:
                        pe.wait_ge(bias_ev, g - 3)
                    for c in range(4):
                        kc = 4 * g + c
                        sel = kt[0:63, C_SEL + 63 - kc:C_SEL + 191 - kc]
                        mm = pe.matmul(ps[:, g % 4, 112 * c:112 * c + 112], sel, rcol[:, :], start=True, stop=True)
                    mm.then_inc(bias_mm, 1)

            bias_products(range(16))
            pe.wait_ge(ada_in[3], 16)
            pe.wait_ge(csil_ok, 1)
            for i in (2, 3):
                for k in range(K):
                    pe.matmul(ps[:, 7, 12 + i:13 + i], adaA[3][:, k, P * i:P * i + P], csil[:, k:k + 1], start=(k == 0), stop=(k == K - 1))
            pe.wait_ge(ada_acc, 4)
            for c in range(14):
                mm = pe.matmul(ps[:, 7, c:c + 1], acc_a[:, c // 4, P * (c % 4):P * (c % 4) + P], ones[:, 0:1], start=True, stop=True)
            mm.then_inc(modcol_mm, 1)
            def x_transposes(g):
                if g < 8:
                    pe.wait_ge(x_act, 4)
                else:
                    pe.wait_ge(x_pool, 2)
                    pe.wait_ge(x_dve, 2)
                if g >= 3:
                    pe.wait_ge(xT_f, g - 2)
                    pe.wait_ge(h_high, (g - 2) // 4)
                for q in range(4):
                    mm = pe.transpose(ps[:, 4 + g % 3, P * q:P * q + P], xs[:, 4 * (g // 8) + q, P * (g % 8):P * (g % 8) + P], ident)
                mm.then_inc(xT_mm, 1)

            for g in range(8):
                x_transposes(g)

            def project(t, k, b):
                return three(ps[:, t % 4, 0:CH], hh[:, k, P * t:P * t + P], hl[:, k, P * t:P * t + P],
                             wh[b][:, k, :], wl[b][:, k, :], k == 0, k == K - 1)

            def tokens_major(n, b):
                pe.wait_ge(win_hi, n + 1)
                pe.wait_ge(win_lo, n + 1)
                for t in range(T):
                    pe.wait_ge(proj_out, 8 * n + (t - 3))
                    for k in range(K):
                        mm = project(t, k, b)
                    mm.then_inc(proj_mm, 1)

            pe.wait_ge(win_hi, 1)
            pe.wait_ge(win_lo, 1)
            pe.wait_ge(bias_ev, 16)
            for k in range(K):
                pe.wait_ge(h_split, k + 1)
                for t in range(2):
                    mm = project(t, k, 0)
                    if k == K - 1:
                        mm.then_inc(proj_mm, 1)
                if k >= 2:
                    x_transposes(8 + k - 2)
            for t in range(2, T):
                if t >= 4:
                    pe.wait_ge(proj_out, t - 3)
                for k in range(K):
                    if t == 4:
                        pe.wait_ge(h_split, 8 + k + 1)
                    mm = project(t, k, 0)
                    if t == 2 and k < 2:
                        x_transposes(16 - 2 + k)
                mm.then_inc(proj_mm, 1)
            with pe.Fori(0, 2) as i:
                for u in range(2):
                    tokens_major(2 * i + (1 + u), (1 + u) % 2)
            pe.wait_ge(proj_out, 24)
            for g in range(12):
                if g >= 4:
                    pe.wait_ge(swT_ev, g - 3)
                for q in range(4):
                    src = tmq[:, 4 * (g % 2) + q, P * (g // 2):P * (g // 2) + P] if g < 8 else tmk[:, 4 * (g % 2) + q, P * (g // 2 - 4):P * (g // 2 - 3)]
                    mm = pe.transpose(ps[:, 4 + g % 4, P * q:P * q + P], src, ident)
                mm.then_inc(swT_mm, 1)
            with pe.Fori(0, 2) as i:
                for u in range(2):
                    b = (1 + u) % 2
                    pe.wait_ge(win_hi, 2 * i + (6 + u))
                    pe.wait_ge(win_lo, 2 * i + (6 + u))
                    for g in range(4):
                        cols, toks = slice(P * (g // 2), P * (g // 2) + P), slice(512 * (g % 2), 512 * (g % 2) + 512)
                        pe.wait_ge(proj_out, 8 * i + (40 + 4 * u + g - 3))
                        for k in range(K):
                            mm = three(ps[:, g, :], wh[b][:, k, cols], wl[b][:, k, cols], hh[:, k, toks], hl[:, k, toks], k == 0, k == K - 1)
                        mm.then_inc(proj_mm, 1)

            def qk(n, u0, s0, window, orders):
                a, j = n // 2, n % 2
                first, width = window(a)
                pe.wait_ge(staged, s0 + needed(window, orders, a))
                if n >= 2 or not isinstance(u0, int) or u0 > 0:
                    pe.wait_ge(logits_ok, u0 + (n - 1))
                for c0, c1 in [(0, min(width, 512))] + [(512, width)] * (width > 512):
                    mm = pe.matmul(banks(2 * j)[:, c0:c1], qz[:, j, P * a:P * a + P], ks[:, first + c0:first + c1], start=True, stop=True)
                mm.then_inc(qk_mm, 1)

            def weigh(n, u0, hp, window, values):
                j, (first, width) = n % 2, window(n // 2)
                nb = -(-width // P)
                pe.wait_ge(pt_ok, u0 + (n + 1))
                if n >= 2 or not isinstance(u0, int) or u0 > 0:
                    pe.wait_ge(o_ok, u0 + (n - 1))
                for i in range(nb):
                    w = min(P, width - P * i)
                    mm = pe.matmul(ps[:, 6 + j, 0:HD], pt[j][0:w, P * i:P * i + P], values(hp, first // P + i, j, w),
                                   start=(i == 0), stop=(i == nb - 1))
                mm.then_inc(pv_mm, 1)

            def attention(pair, hp, window, values, orders, ahead, before):
                u0, s0 = 16 * pair, STEPS * pair
                for n in range(16):
                    width = window(n // 2)[1]
                    nb = -(-width // P)
                    pe.wait_ge(exp_ok, u0 + (n + 1))
                    turns = 2 if nb <= 3 else 1
                    if n >= turns or before:
                        pe.wait_ge(pt_ok, u0 + (n + 1 - turns))
                    for i in range(nb):
                        w = min(P, width - P * i)
                        mm = pe.transpose(ps[0:w, T_bank(n, nb) + i // 4, P * (i % 4):P * (i % 4) + P], pb[n % 4][:, P * i:P * i + w], ident)
                    mm.then_inc(pT_mm, 1)
                    if n + 2 < 16:
                        qk(n + 2, u0, s0, window, orders)
                    elif ahead:
                        qk(n - 14, u0 + 16, s0 + STEPS, *ahead)
                    if n >= 1:
                        weigh(n - 1, u0, hp, window, values)
                    elif before:
                        weigh(15, u0 - 16, *before)
                    if n == 15:
                        pe.wait_ge(adaC_used, 2 * pair + 2)
                        pe.wait_ge(brow_in, 16 * pair + 16)
                        pe.matmul(mod_bank(window), ones, acc_c[:, :, :].rearrange("p c n -> p (c n)"), start=True, stop=False)
                        pe.matmul(mod_bank(window), ones[0:1, :], b_row[0:1, :], start=False, stop=True).then_inc(mod_mm, 1)

            def sw_values(hp, t, j, w):
                return svt[0:w, t, ds(HD * (hp // 2), HD)]

            def na_values(hp, t, j, w):
                return vna[0:w, t, ds(P * hp + HD * j, HD)]

            pe.wait_ge(proj_out, 56)
            for n in range(2):
                qk(n, 0, 0, sw_win, [STAGE_SW])
            SW, NA = (sw_win, [STAGE_SW]), (na_win, [STAGE_SW, STAGE_NA])
            sw, na = (sw_win, sw_values), (na_win, na_values)
            attention(0, 0, *sw, [STAGE_SW], SW, None)
            with pe.Fori(1, 3) as hp:
                attention(hp, hp, *sw, [STAGE_SW], SW, (hp - 1, *sw))
            attention(3, 3, *sw, [STAGE_SW], NA, (2, *sw))
            attention(4, 0, *na, NA[1], NA, (3, *sw))
            with pe.Fori(1, 3) as hp:
                attention(hp + 4, hp, *na, NA[1], NA, (hp - 1, *na))
            attention(7, 3, *na, NA[1], None, (2, *na))
            weigh(15, 112, 3, *na)
            def o_transposes(t):
                pe.wait_ge(os_ok, t + 1)
                if t >= 1:
                    pe.wait_ge(m_hi, t)
                    pe.wait_ge(m_lo, t)
                for k in range(K):
                    mm = pe.transpose(ps[:, k // 4, P * (k % 4):P * (k % 4) + P], osc[:, P * k:P * k + P], ident)
                mm.then_inc(oT_mm, 1)

            def h2_transposes(t):
                pe.wait_ge(mod_ok, 8)
                pe.wait_ge(h2_ok, t + 1)
                for k in range(K):
                    mm = pe.transpose(ps[:, 4 + k // 4, P * (k % 4):P * (k % 4) + P], h2[t % 2][:, P * k:P * k + P], ident)
                mm.then_inc(h2T_mm, 1)

            def logits(t):
                pe.wait_ge(h2T_ok, t + 1)
                if t >= 2:
                    pe.wait_ge(lg_ok, t - 1)
                for k in range(K):
                    mm = pe.matmul(ps[:, 6 + t % 2, 0:36], h2T[:, k, :], wrt[:, k, :], start=(k == 0), stop=(k == K - 1))
                mm.then_inc(lg_mm, 1)

            o_transposes(0)
            pe.wait_ge(router_in, 16)
            for t in range(T):
                pe.wait_ge(m_hi, t + 1)
                if t >= 1:
                    pe.wait_ge(mix_out, t)
                for c in range(4):
                    if c == 2 and t + 1 < T:
                        o_transposes(t + 1)
                    if t == 0:
                        pe.wait_ge(wout_hi, c + 1)
                        pe.wait_ge(wout_lo, c + 1)
                    dst = ps[:, 2 + c // 2, CH * (c % 2):CH * (c % 2) + CH]
                    for k in range(K):
                        if c == 0:
                            pe.matmul(dst, mh[t % 2][:, k, :], woh[c][:, k, :], start=(k == 0), stop=False)
                            pe.matmul(dst, mh[t % 2][:, k, :], wol[c][:, k, :], start=False, stop=False)
                        else:
                            mm = three(dst, mh[t % 2][:, k, :], ml[t % 2][:, k, :], woh[c][:, k, :], wol[c][:, k, :], k == 0, k == K - 1)
                    if c == 0:
                        pe.wait_ge(m_lo, t + 1)
                        for k in range(K):
                            pe.matmul(dst, ml[t % 2][:, k, :], woh[c][:, k, :], start=False, stop=(k == K - 1))
                mm.then_inc(mix_mm, 1)
                if t >= 2:
                    logits(t - 2)
                if t >= 1:
                    h2_transposes(t - 1)
            logits(T - 2)
            h2_transposes(T - 1)
            logits(T - 1)

            pe.wait_ge(r_pre, 1)
            pe.matmul(ps[:, 7, 0:256], tri, rw[:, R_A:R_A + 256], start=True, stop=False)
            pe.matmul(ps[:, 7, 0:256], ones, rw[:, R_C:R_C + 256], start=False, stop=True)
            pe.matmul(ps[:, 7, 256:288], ones, rw[:, R_C + 256:R_C + 288], start=True, stop=True).then_inc(pos_mm, 1)
            for i in range(16):
                if i % 8 == 0:
                    pe.wait_ge(lane_ok, i // 8 + 1)
                    pe.wait_ge(rec_ok, i // 8 + 1)
                mm = pe.matmul(ps[:, 7, 0:2 * MAXB], lanes[:, i, :], recs[:, i, :], start=(i == 0), stop=(i == 15))
            mm.then_inc(tab_mm, 1)

            pe.wait_ge(np_ok, 1)
            n_pairs = pe.value_load(btab[0:1, MAXB:MAXB + 1], min_val=NE // 2 - 2, max_val=MAXB // 2 - 2) + 2

            def x_T(u, b, landed):
                pe.wait_ge(xg_in[u], landed)
                pe.wait_ge(xgT_a, b)
                pe.wait_ge(xgT_b, b)
                for k in range(K):
                    mm = pe.transpose(ps[:, 2 + k // 4, P * (k % 4):P * (k % 4) + P], xg[u][:, P * k:P * k + P], ident)
                mm.then_inc(xgT_mm, 1)

            def gate_up(u, b, landed, used):
                pe.wait_ge(xgT_a, b + 1)
                pe.wait_ge(xgT_b, b + 1)
                pe.wait_ge(gu_in[u], landed)
                pe.wait_ge(hid_ok, used)
                for k in range(K):
                    mm = pe.matmul(ps[:, u, :], xgT[u][:, k, :], wgu[u][:, k, :], start=(k == 0), stop=(k == K - 1))
                mm.then_inc(gu_mm, 1)

            def hid_T(u, b):
                pe.wait_ge(hid_ok, b + 1)
                pe.wait_ge(hidT_ok, b)
                for k in range(2):
                    mm = pe.transpose(ps[:, 4, P * k:P * k + P], hid[u][:, P * k:P * k + P], ident)
                mm.then_inc(hidT_mm, 1)

            def down(u, b, landed):
                pe.wait_ge(hidT_ok, b + 1)
                pe.wait_ge(dn_in[u], landed)
                pe.wait_ge(yg_a, b)
                pe.wait_ge(yg_b, b)
                for i in range(2):
                    for k in range(2):
                        mm = pe.matmul(ps[:, 5 + i, :], hidT[u][:, k, :], wd[u][:, k, 512 * i:512 * i + 512], start=(k == 0), stop=(k == 1))
                mm.then_inc(dn_mm, 1)

            x_T(0, 0, 16)
            gate_up(0, 0, 16, 0)
            x_T(1, 1, 16)
            with pe.Fori(1, n_pairs) as j:
                for u in (1, 0):
                    b = 2 * j - u
                    gate_up(u, b, 16 * j + (16 - 16 * u), b - 1)
                    hid_T(1 - u, b - 1)
                    x_T(1 - u, b + 1, 16 * j + 16)
                    down(1 - u, b - 1, 16 * j)
            last = 2 * n_pairs - 1
            gate_up(1, last, 16 * n_pairs, last - 1)
            for u in range(2):
                hid_T(u, last - 1 + u)
                down(u, last - 1 + u, 16 * n_pairs)

        @block.scalar
        def _(act):
            squares = [0]

            def load_table(func, i):
                act.activation(small[:, 184 + i:185 + i], eps, func)

            def square_sum(dst, src, junk=junk):
                if squares[0]:
                    act.wait_ge(squared, squares[0])
                squares[0] += 1
                act.activation(junk[:, 0:src.shape[-1]], src, ACT.Square, accum_out=dst).then_inc(squared, 1)

            def roots(dst, src, n):
                act.wait_ge(squared, squares[0])
                return act.activation(dst, src, ACT.Sqrt, bias=eps, scale=1.0 / n)

            act.wait_ge(vec_in, 48)
            act.activation(csil, vt[:, V_C:V_C + 8], ACT.Silu).then_inc(csil_ok, 1)
            for t in range(T):
                act.wait_ge(x_in[t // 4], 16)
                square_sum(xss[:, t:t + 1], xs[:, t, :], junk_x)
                if t % 4 == 3:
                    act.wait_ge(const_in, 16)
                    half = slice(t - 3, t + 1)
                    roots(xrt[:, half], xss[:, half], D).then_inc(x_root, 1)
                if t == 3:
                    act.wait_ge(xr_ok, 1)
                    for q in range(4):
                        act.activation(xs[:, q, :], xs[:, q, :], ACT.Copy, scale=xrs[:, q:q + 1]).then_inc(x_act, 1)
            def win_round(n):
                act.wait_ge(win_in[n % 2], 16 * (n // 2) + 16)
                if n >= 2:
                    act.wait_ge(proj_mm, 8 * (n - 1) if n <= 6 else 40 + 4 * (n - 6))
                else:
                    act.wait_ge(ada_acc, n + 1)
                act.activation(wh[n % 2][:, :, :], wf[n % 2][:, :, :], ACT.Copy).then_inc(win_hi, 1)

            win_round(0)
            act.wait_ge(cols_ok, 1)
            for g in range(16):
                act.wait_ge(xT_mm, g + 1)
                if g >= 4:
                    act.wait_ge(h_split, g - 3)
                k = g % 8
                of_x = dict(bias=col_shift[:, k:k + 1], scale=col_scale[:, k:k + 1])
                if g % 4 == 3:
                    act.activation(hh[:, k, 512 * (g // 8):512 * (g // 8) + 512], ps[:, 4 + g % 3, :], ACT.Identity, **of_x).then_inc(h_high, 1)
                act.activation(hf[g % 4][:, :], ps[:, 4 + g % 3, :], ACT.Identity, **of_x).then_inc(xT_f, 1)
                if g == 7:
                    win_round(1)

            for n in range(N_IN):
                if 1 <= n < N_IN - 1:
                    win_round(n + 1)
                if n == 3:
                    act.wait_ge(proj_out, 24)
                    act.wait_ge(bias_saved, 16 * 20)
                if n in (3, 4):
                    for t in range(T):
                        act.wait_ge(proj_mm, 8 * n + t + 1)
                        act.copy(vna[:, t, CH * (n - 3):CH * (n - 3) + CH], ps[:, t % 4, 0:CH]).then_inc(proj_out, 1)
                if n == 4:
                    for g in range(12):
                        act.wait_ge(swT_mm, g + 1)
                        dst = qall[:, g // 2, :] if g < 8 else kall[:, g // 2 - 4, :]
                        act.copy(dst[:, 512 * (g % 2):512 * (g % 2) + 512], ps[:, 4 + g % 4, :]).then_inc(swT_ev, 1)
                if n >= 5:
                    for g in range(4):
                        act.wait_ge(proj_mm, 41 + 4 * (n - 5) + g)
                        pair = 2 * ((n - 5) % 2) + g // 2
                        dst = qall[:, 4 + pair, :] if n < 7 else kall[:, 2 + pair, :]
                        act.copy(dst[:, 512 * (g % 2):512 * (g % 2) + 512], ps[:, g, :]).then_inc(proj_out, 1)

            def square_half(hp, i, done):
                act.wait_ge(squared, 2 * hp + (done + i))
                src = ot[:, ds(2 * hp + i, 1), 512:1024].rearrange("p a n -> p (a n)")
                act.activation(junk[:, 0:512], src, ACT.Square,
                               accum_out=oss[:, ds(2 * hp + (8 + i), 1)]).then_inc(squared, 1)

            def pt_copy(m, u0, window, slides):
                w = window(m // 2)[1]
                act.wait_ge(pT_mm, u0 + (m + 1))
                if m >= 2 or not isinstance(u0, int) or u0 > 0:
                    act.wait_ge(pv_mm, u0 + (m - 1))
                n4 = P * -(-min(w, 512) // P)
                last = act.copy(pt[m % 2][:, 0:n4], ps[:, T_bank(m, n4 // P), 0:n4])
                if w > 512:
                    last = act.copy(pt[m % 2][0:64, 512:640], ps[0:64, 5, 0:P])
                last.then_inc(pt_ok, 1)

            def attention(u0, window, slides, before, between=None):
                for n in range(16):
                    if between and n in (5, 12):
                        if n == 5:
                            act.wait_ge(o_ok, 64)
                        between(n // 12)
                    w = window(n // 2)[1]
                    act.wait_ge(logits_ok, u0 + (n + 1))
                    row = pb[n % 4][:, 0:w + slides]
                    act.activation(row, row, ACT.Exp, bias=asm[:, n:n + 1], scale=-1.0, accum_out=asm[:, 16 + n:17 + n]).then_inc(exp_ok, 1)
                    if n >= 1 and not on_dve(n - 1, slides):
                        pt_copy(n - 1, u0, window, slides)
                    elif n == 0 and before and not on_dve(15, before[1]):
                        pt_copy(15, u0 - 16, *before)

            attention(0, sw_win, True, None)
            with act.Fori(1, 4) as hp:
                attention(16 * hp, sw_win, True, (sw_win, True))
            done = squares[0]
            attention(64, na_win, False, (sw_win, True), lambda i: square_half(0, i, done))
            with act.Fori(1, 4) as hp:
                attention(16 * hp + 64, na_win, False, (na_win, False), lambda i: square_half(hp, i, done))
            squares[0] = done + T
            load_table(ACT.Sqrt, 0)

            def o_roots(t):
                act.wait_ge(o_ok, 114 + 2 * t)
                square_sum(oss[:, t:t + 1], ot[:, t, 0:512])
                roots(ort.rearrange("p (g t) -> p g t", g=2)[:, :, t], oss.rearrange("p (g t) -> p g t", g=2)[:, :, t], 512).then_inc(o_root, 1)

            def mix_round(t):
                act.wait_ge(oT_mm, t + 1)
                if t >= 2:
                    act.wait_ge(mix_mm, t - 1)
                act.activation(mh[t % 2][:, :, :].rearrange("p k n -> p (k n)"), banks(0), ACT.Copy).then_inc(m_hi, 1)

            o_roots(0)
            mix_round(0)
            o_roots(1)
            o_roots(2)
            for t in range(T):
                if t + 1 < T:
                    mix_round(t + 1)
                if t + 3 < T:
                    o_roots(t + 3)
                act.wait_ge(mix_mm, t + 1)
                if t + 1 < T:
                    act.copy(x1[:, t, :], banks(2)).then_inc(mix_out, 1)
                    act.wait_ge(mix_out, t + 1)
                square_sum(mst[:, t:t + 1], x1[:, t, :] if t + 1 < T else banks(2))
                roots(mst[:, 8 + t:9 + t], mst[:, t:t + 1], D).then_inc(mix_root, 1)
                act.wait_ge(x1_ok, t + 1)
                square_sum(gst[:, t:t + 1], x1[:, t, :])
                roots(gst[:, 8 + t:9 + t], gst[:, t:t + 1], D).then_inc(x1_root, 1)
                if t >= 1:
                    act.wait_ge(h2T_mm, t)
                    if t >= 2:
                        act.wait_ge(lg_mm, t - 1)
                    act.copy(h2T[:, :, :].rearrange("p k n -> p (k n)"), banks(4)).then_inc(h2T_ok, 1)
            act.wait_ge(h2T_mm, T)
            act.wait_ge(lg_mm, T - 1)
            act.copy(h2T[:, :, :].rearrange("p k n -> p (k n)"), banks(4)).then_inc(h2T_ok, 1)
            load_table(ACT.Exp, 3)
            act.wait_ge(r_exp_in, 1)
            act.activation(rw[:, R_EX:R_EX + 40], rw[:, R_EI:R_EI + 40], ACT.Exp).then_inc(r_exp, 1)

            load_table(ACT.Silu, 1)

            act.wait_ge(np_ok, 1)
            n_pairs = act.value_load(btab[0:1, MAXB:MAXB + 1], min_val=NE // 2 - 2, max_val=MAXB // 2 - 2) + 2

            def x_T(u, b):
                act.wait_ge(xgT_mm, b + 1)
                act.wait_ge(gu_mm, b - 1 if not isinstance(b, int) or b > 1 else 0)
                act.copy(xgT[u][:, 4:8, :].rearrange("p k n -> p (k n)"), ps[:, 3, :]).then_inc(xgT_b, 1)

            def silu(u, b):
                act.wait_ge(gu_mm, b + 1)
                act.activation(sg[u][:, :], ps[:, u, 0:FF], ACT.Silu).then_inc(sg_ok, 1)

            def gated(u, b, stored):
                act.wait_ge(dn_mm, b + 1)
                act.wait_ge(y_put[u], stored)
                act.activation(yg[u][:, 0:512], ps[:, 5, :], ACT.Copy, scale=tab[:, ds(b, 1), 2:3].bitcast(F32).rearrange("p a c -> p (a c)")).then_inc(yg_a, 1)

            act.wait_ge(tab_in, 1)
            x_T(0, 0)
            silu(0, 0)
            x_T(1, 1)
            with act.Fori(1, n_pairs) as j:
                for u in (1, 0):
                    b = 2 * j - u
                    silu(u, b)
                    x_T(1 - u, b + 1)
                    gated(1 - u, b - 1, 16 * j - 16)
            last = 2 * n_pairs - 1
            silu(1, last)
            gated(0, last - 1, 16 * n_pairs - 16)
            gated(1, last, 16 * n_pairs - 16)
            load_table(ACT.Sqrt, 2)
            for t in range(T):
                act.wait_ge(y_sum[t % 2], t // 2 + 1)
                square_sum(fst[:, t:t + 1], yab[:, t, 0, :], junk_x)
                roots(fst[:, 8 + t:9 + t], fst[:, t:t + 1], D).then_inc(y_root, 1)

        @block.vector
        def _(dve):
            chain = [0, 0]

            def mark(ins):
                chain[0] += 1
                ins.then_inc(dve_chain, 1)

            def settle():
                dve.wait_ge(dve_chain, chain[1] + chain[0])

            def link(ins):
                mark(ins)
                settle()

            def looped(i, per, before):
                chain[0], chain[1] = before, per * i

            def weigh(acc, w, k):
                settle()
                if k == 0:
                    mark(dve.tensor_scalar(acc, w[:, 0, :], csil[:, 0:1], None, ALU.mult))
                else:
                    mark(dve.scalar_tensor_tensor(acc, w[:, k, :], csil[:, k:k + 1], acc, ALU.mult, ALU.add))

            dve.wait_ge(const_in, 16)
            dve.wait_ge(vec_in, 48)
            link(dve.tensor_scalar(nsink[:, :], nsink[:, :], -1.0, None, ALU.mult))
            def bias_group(g):
                dve.wait_ge(bias_mm, g + 1)
                table = bias_b[:, 0:14, :, 4 * g:4 * g + 4].rearrange("p m h c -> p (m h) c")
                src = ps[:, g % 4, 0:448].rearrange("p (c m) -> p m c", c=4)
                mask = bc(kt[:, C_NAM + 4 * g:C_NAM + 4 * g + 4].unsqueeze(1), 1, 112)
                dve.scalar_tensor_tensor(table, src, float(HD) ** 0.5, mask, ALU.mult, ALU.add).then_inc(bias_ev, 1)

            dve.wait_ge(csil_ok, 1)
            def mix_sums(c, n=512):
                dve.wait_ge(ada_in[c], 16)
                for k in range(K):
                    weigh(acc_a[:, c, 0:n], adaA[c][:, :, 0:n], k)
                settle()
                dve.sem_inc(ada_acc, 1)

            def over_root(half):
                dve.wait_ge(x_root, half + 1)
                dve.reciprocal(xrs[:, 4 * half:4 * half + 4], xrt[:, 4 * half:4 * half + 4]).then_inc(xr_ok, 1)

            def win_rest(n):
                dve.wait_ge(win_hi, n + 1)
                dve.tensor_tensor(wl[n % 2][:, :, :], wf[n % 2][:, :, :], wh[n % 2][:, :, :].bitcast(F32), ALU.subtract).then_inc(win_lo, 1)

            for c in range(3):
                for g in range(4 * c, 4 * c + 4):
                    bias_group(g)
                if c == 2:
                    over_root(0)
                mix_sums(c)
            mix_sums(3, 256)
            for g in range(12, 16):
                bias_group(g)
            over_root(1)
            dve.wait_ge(xr_ok, 2)
            for t in range(6, T):
                dve.tensor_scalar(xs[:, t, :], xs[:, t, :], xrs[:, t:t + 1], None, ALU.mult).then_inc(x_dve, 1)
            dve.wait_ge(modcol_mm, 1)
            link(dve.tensor_tensor(mcol, ps[:, 7, 0:16], vt[:, V_BADA:V_BADA + 16], ALU.add))
            dve.tensor_copy(col_shift, mcol[:, 0:8])
            link(dve.scalar_tensor_tensor(col_scale, mcol[:, 8:16], 1.0, vt[:, V_G:V_G + 8], ALU.add, ALU.mult))
            dve.sem_inc(cols_ok, 1)
            for g in range(16):
                k, cols = g % 8, slice(512 * (g // 8), 512 * (g // 8) + 512)
                dve.wait_ge(xT_f, g + 1)
                if g % 4 == 3:
                    dve.wait_ge(h_high, g // 4 + 1)
                else:
                    link(dve.tensor_copy(hh[:, k, cols], hf[g % 4][:, :]))
                dve.tensor_tensor(hl[:, k, cols], hf[g % 4][:, :], hh[:, k, cols].bitcast(F32), ALU.subtract).then_inc(h_split, 1)

            def rope(src, heads, t, dst):
                cos = bc(kt[:, ds(C_COS + 64 * t, 64)].unsqueeze(1), 1, heads)
                sin = bc(kt[:, ds(C_SIN + 64 * t, 64)].unsqueeze(1), 1, heads)
                n = heads * HD
                a, b = (r[:, 0:n].rearrange("p (h c) -> p h c", c=HD) for r in (rt1, rt2))
                dve.tensor_tensor(a, src, cos, ALU.mult)
                dve.tensor_tensor(b[:, :, 0:32], src[:, :, 32:64], sin[:, :, 0:32], ALU.mult)
                link(dve.tensor_tensor(b[:, :, 32:64], src[:, :, 0:32], sin[:, :, 32:64], ALU.mult))
                if heads == 2:
                    for r in range(2):
                        last = dve.tensor_tensor(dst[:, :, r, :], a, b, ALU.add)
                    return last
                return dve.tensor_tensor(dst, a, b, ALU.add)

            for n in range(3):
                if n == 1:
                    dve.wait_ge(bias_saved, 16 * 20)
                if n == 1:
                    dve.wait_ge(win_lo, 2)
                if n >= 1:
                    win_rest(n + 1)
                before = chain[0]
                with dve.Fori(0, 2) as i:
                    looped(i, 8 if n == 0 else 4, before)
                    for q in range(4):
                        t = 4 * i + q
                        dve.wait_ge(proj_mm, 4 * i + (8 * n + q + 1))
                        dve.wait_ge(proj_out, 4 * i + (8 * n + q))
                        if n == 0:
                            link(dve.tensor_copy(svt[:, ds(t, 1), :].rearrange("p a n -> p (a n)"), ps[:, q, P:2 * P]))
                            dst = tmk[:, ds(t, 1), :].rearrange("p a (h r c) -> p (a h) r c", h=2, r=2)
                            rope(ps[:, q, 0:P].rearrange("p (h c) -> p h c", c=HD), 2, t, dst).then_inc(proj_out, 1)
                        else:
                            dst = tmq[:, ds(t, 1), CH * (n - 1):CH * n].rearrange("p a (h c) -> p (a h) c", c=HD)
                            rope(ps[:, q, 0:CH].rearrange("p (h c) -> p h c", c=HD), 4, t, dst).then_inc(proj_out, 1)
                per = chain[0] - before
                chain[0], chain[1] = before + 2 * per, 0
            for n in range(4, N_IN):
                win_rest(n)

            def one_over(m, u0):
                dve.wait_ge(exp_ok, u0 + (m + 1))
                mark(dve.reciprocal(asm[:, 48 + m:49 + m], asm[:, 16 + m:17 + m]))

            def scale_out(m, u0, hp, window, slides):
                a, j = m // 2, m % 2
                settle()
                dve.wait_ge(pv_mm, u0 + (m + 1))
                col = (512 if slides else 0) + HD * j
                dve.tensor_scalar(ot[:, a, ds(P * hp + col, HD)], ps[:, 6 + j, 0:HD], asm[:, 48 + m:49 + m], None, ALU.mult).then_inc(o_ok, 1)

            def pt_copy(m, u0, window):
                w = window(m // 2)[1]
                dve.wait_ge(pT_mm, u0 + (m + 1))
                dve.wait_ge(pv_mm, u0 + (m - 1))
                n4 = P * -(-min(w, 512) // P)
                last = dve.tensor_copy(pt[m % 2][:, 0:n4], ps[:, T_bank(m, n4 // P), 0:n4])
                if w > 512:
                    last = dve.tensor_copy(pt[m % 2][0:64, 512:640], ps[0:64, 5, 0:P])
                last.then_inc(pt_ok, 1)

            def bias_of(a, j):
                _, n, s = na_window(a)
                return bias[:, s:s + n, HD * j:HD * j + HD]

            def mask_of(b, j):
                _, n, s = sw_window(b)
                return kt[:, C_SWM + P * s:C_SWM + P * (s + n)]

            def mod_row(pair, hp, window, slides):
                dve.wait_ge(rows_in, 48)
                dve.wait_ge(mod_mm, pair + 1)
                half = mods[:, :, :].rearrange("p r n -> p (r n)")[:, ds(512 * pair, 512)]
                plus = 0.0 if slides else kt[:, ds(C_PLUS + hp, 1)]
                dve.scalar_tensor_tensor(half, mod_bank(window), plus, half, ALU.add, ALU.mult).then_inc(mod_ok, 1)

            def attention(pair, hp, window, slides, before):
                u0 = 16 * pair
                if slides:
                    if before:
                        dve.wait_ge(logits_ok, u0)
                    link(dve.tensor_copy(asm[:, 64:66], nsink[:, ds(2 * hp, 2)]))
                for n in range(16):
                    a, j = n // 2, n % 2
                    w = window(a)[1]
                    if not slides and n in (0, 4, 12):
                        dve.wait_ge(bias_in[(0, 4, 12).index(n)], 16 * hp + 16)
                    if n >= 3:
                        one_over(n - 3, u0)
                    elif before:
                        one_over(n + 13, u0 - 16)
                    dve.wait_ge(qk_mm, u0 + (n + 1))
                    if n >= 4 or before:
                        dve.wait_ge(pT_mm, u0 + (n - 3))
                    dve.sem_inc(logits_due, 1)
                    if slides:
                        dve.tensor_copy(pb[n % 4][:, w:w + 1], asm[:, 64 + j:65 + j])
                    sh = (lambda ap: ap) if slides else (lambda ap: ap.rearrange("p (r c) -> p r c", c=GRID_W))
                    dve.tensor_tensor_reduce(sh(pb[n % 4][:, 0:w]), sh(banks(2 * j)[:, 0:w]), (mask_of if slides else bias_of)(a, j),
                                             -(float(HD) ** -0.5), asm[:, 64 + j:65 + j] if slides else 3.0e38, ALU.add, ALU.min,
                                             asm[:, n:n + 1]).then_inc(logits_ok, 1)
                    if n == 1 and before:
                        mod_row(pair - 1, *before)
                    if n >= 3:
                        scale_out(n - 3, u0, hp, window, slides)
                    elif before:
                        scale_out(n + 13, u0 - 16, *before)
                    if n >= 1 and on_dve(n - 1, slides):
                        pt_copy(n - 1, u0, window)
                    elif n == 0 and before and on_dve(15, before[2]):
                        pt_copy(15, u0 - 16, before[1])
                    if 2 <= n < 14:
                        for m in (2 * n - 4, 2 * n - 3) if n < 6 else (n + 2,):
                            c, k = m // K, m % K
                            if k == 0:
                                dve.wait_ge(adaC_in[c], 16 * pair + 16)
                            weigh(acc_c[:, c, :], adaC[c], k)
                        if n in (5, 13):
                            settle()
                            dve.sem_inc(adaC_used, 1)

            dve.wait_ge(proj_out, 56)
            dve.memset(mods[:, 1, :], 1.0)
            attention(0, 0, sw_win, True, None)
            before, per = chain[0], 16 + 1 + 16
            with dve.Fori(1, 4) as hp:
                looped(hp - 1, per, before)
                attention(hp, hp, sw_win, True, (hp - 1, sw_win, True))
                assert chain[0] - before == per, chain[0] - before
            chain[0], chain[1] = before + 3 * per, 0
            attention(4, 0, na_win, False, (3, sw_win, True))
            before, per = chain[0], 16 + 16
            with dve.Fori(1, 4) as hp:
                looped(hp - 1, per, before)
                attention(hp + 4, hp, na_win, False, (hp - 1, na_win, False))
                assert chain[0] - before == per, chain[0] - before
            chain[0], chain[1] = before + 3 * per, 0
            pt_copy(15, 112, na_win)
            def o_scale(t):
                if t >= 1:
                    dve.wait_ge(oT_mm, t)
                dve.wait_ge(o_root, t + 1)
                halves = lambda ap: ap.rearrange("p (g t) -> p g t", g=2)[:, :, t]
                link(dve.reciprocal(halves(ors), halves(ort)))
                for g in range(2):
                    cols = slice(512 * g, 512 * g + 512)
                    last = dve.scalar_tensor_tensor(osc[:, cols], ot[:, t, cols], ors[:, 8 * g + t:8 * g + t + 1], beta_b[:, cols], ALU.mult, ALU.mult)
                last.then_inc(os_ok, 1)

            for m in range(13, 16):
                one_over(m, 112)
                if m == 15:
                    dve.wait_ge(beta_in, 16)
                    o_scale(0)
                scale_out(m, 112, 3, na_win, False)

            def mix_rest(t):
                dve.wait_ge(m_hi, t + 1)
                dve.tensor_tensor(ml[t % 2][:, :, :].rearrange("p k n -> p (k n)"), banks(0),
                                  mh[t % 2][:, :, :].bitcast(F32).rearrange("p k n -> p (k n)"), ALU.subtract).then_inc(m_lo, 1)

            mod_row(7, 3, na_win, False)
            mix_rest(0)
            o_scale(1)
            for t in range(T):
                if t + 1 < T:
                    mix_rest(t + 1)
                if t + 2 < T:
                    o_scale(t + 2)
                xt, ht, x1t = xb[t % 2][:, :], h2[t % 2][:, :], x1[:, t, :]
                dve.wait_ge(mix_root, t + 1)
                link(dve.reciprocal(mst[:, 16 + t:17 + t], mst[:, 8 + t:9 + t]))
                mix = x1t if t + 1 < T else banks(2)
                link(dve.scalar_tensor_tensor(x1t, mix, mst[:, 16 + t:17 + t], mods[:, 0, :], ALU.mult, ALU.mult))
                dve.wait_ge(xb_in[t % 2], 16 * (t // 2) + 16)
                dve.tensor_tensor(x1t, x1t, xt, ALU.add).then_inc(x1_ok, 1)
                if t >= 1:
                    dve.wait_ge(lg_mm, t - 1) if t >= 2 else None
                    if t >= 2:
                        dve.tensor_copy(lg[:, t - 2, :], ps[:, 6 + t % 2, 0:36]).then_inc(lg_ok, 1)
                dve.wait_ge(x1_root, t + 1)
                link(dve.reciprocal(gst[:, 16 + t:17 + t], gst[:, 8 + t:9 + t]))
                if t >= 2:
                    dve.wait_ge(h2_saved[t % 2], 16 * (t // 2))
                    dve.wait_ge(h2T_mm, t - 1)
                link(dve.scalar_tensor_tensor(ht, x1t, gst[:, 16 + t:17 + t], mods[:, 2, :], ALU.mult, ALU.mult))
                dve.tensor_tensor(ht, ht, mods[:, 1, :], ALU.add).then_inc(h2_ok, 1)
            def r(at, *dims):
                n = 1
                for d in dims:
                    n *= d
                ap = rw[:, at:at + n]
                if len(dims) == 2:
                    return ap.rearrange("p (a b) -> p a b", a=dims[0])
                if len(dims) == 3:
                    return ap.rearrange("p (a b c) -> p a b c", a=dims[0], b=dims[1])
                return ap

            def spread(ap, n):
                ap = ap.unsqueeze(len(ap.shape))
                return bc(ap, len(ap.shape) - 1, n)

            iota = kt[:, C_IOTA:C_IOTA + MAXB]
            link(dve.memset(r(R_G, 64), NEG))
            link(dve.memset(r(R_C, NE), 0.0))

            def choose(t0, t1):
                n = t1 - t0
                group, best, other = r(R_G, T, 8)[:, t0:t1, :], r(R_V, T, 8)[:, t0:t1, :], r(R_OG, T, NG)[:, t0:t1, :]
                found = ru[:, 0:64].rearrange("p (t c) -> p t c", c=8)[:, t0:t1, :]
                running = r(R_EM, T, NG, EPG)[:, t0:t1, :, :]
                link(dve.tensor_copy(group[:, :, 0:NG], lg[:, t0:t1, 0:NG]))
                for t in range(n):
                    last = dve.max(best[:, t, :], group[:, t, :])
                link(last)
                for t in range(n):
                    last = dve.max_index(found[:, t, :], best[:, t, :], group[:, t, :])
                link(last)
                link(dve.tensor_copy(r(R_GI + t0, n), found[:, :, 0]))
                dve.tensor_tensor(r(R_EI, T, NG)[:, t0:t1, :], lg[:, t0:t1, 0:NG], spread(best[:, :, 0], NG), ALU.subtract)
                link(dve.tensor_tensor(other, bc(iota[:, 0:NG].unsqueeze(1), 1, n), spread(r(R_GI + t0, n), NG), ALU.is_equal))
                link(dve.tensor_tensor(running, lg[:, t0:t1, NG:].rearrange("p t (g e) -> p t g e", g=NG), spread(other, EPG), ALU.mult))
                link(dve.tensor_scalar(other, other, -1.0, -NEG, ALU.add, ALU.mult))
                link(dve.tensor_tensor(running, running, spread(other, EPG), ALU.add))
                for t in range(t0, t1):
                    last = dve.max(r(R_V, T, 8)[:, t, :], r(R_EM, T, NE)[:, t, :])
                link(last)
                for t in range(t0, t1):
                    last = dve.max_index(ru[:, 8 * t:8 * t + 8], r(R_V, T, 8)[:, t, :], r(R_EM, T, NE)[:, t, :])
                link(last)
                dve.tensor_tensor(r(R_EI + 32 + t0, n), best[:, :, 1], best[:, :, 0], ALU.subtract)
                for j in range(2):
                    last = dve.tensor_copy(r(R_ID + T * j + t0, n), found[:, :, j])
                link(last)
                for j in range(2):
                    last = dve.tensor_tensor(r(R_O + 256 * j + NE * t0, n, NE), bc(iota[:, 0:NE].unsqueeze(1), 1, n), spread(r(R_ID + T * j + t0, n), NE), ALU.is_equal)
                link(last)
                link(dve.tensor_tensor(r(R_A + NE * t0, n * NE), r(R_O + NE * t0, n * NE), r(R_O + 256 + NE * t0, n * NE), ALU.add))
                for t in range(t0, t1):
                    link(dve.tensor_tensor(r(R_C + NE * (t + 1), NE), r(R_C + NE * t, NE), r(R_A + NE * t, NE), ALU.add))

            choose(0, T - 2)
            for t in range(T - 2, T):
                dve.wait_ge(lg_mm, t + 1)
                dve.tensor_copy(lg[:, t, :], ps[:, 6 + t % 2, 0:36]).then_inc(lg_ok, 1)
            dve.wait_ge(lg_ok, T)
            choose(T - 2, T)
            dve.sem_inc(r_exp_in, 1)
            dve.sem_inc(r_pre, 1)
            dve.wait_ge(r_exp, 1)
            link(dve.tensor_reduce(r(R_GW, T), r(R_EX, T, NG), AX.X, ALU.add))
            link(dve.tensor_scalar(r(R_T, T), r(R_EX + 32, T), 1.0, None, ALU.add))
            link(dve.tensor_tensor(r(R_GW, T), r(R_GW, T), r(R_T, T), ALU.mult))
            link(dve.reciprocal(r(R_W, T), r(R_GW, T)))
            link(dve.tensor_tensor(r(R_W + T, T), r(R_W, T), r(R_EX + 32, T), ALU.mult))
            dve.wait_ge(pos_mm, 1)
            pos = ps[:, 7, 0:288]
            for j in range(2):
                last = dve.tensor_tensor(r(R_T + 256 * j, 256), pos[:, 0:256], r(R_O + 256 * j, 256), ALU.mult)
            link(last)
            link(dve.tensor_reduce(r(R_P, 16), r(R_T, 16, NE), AX.X, ALU.add))
            step = kt[:, C_STEP:C_STEP + 7]
            link(dve.tensor_tensor(r(R_T, 16, 7), spread(r(R_P, 16), 7), bc(step.unsqueeze(1), 1, 16), ALU.is_ge))
            link(dve.tensor_reduce(r(R_B, 16), r(R_T, 16, 7), AX.X, ALU.add))
            link(dve.scalar_tensor_tensor(r(R_P, 16), r(R_B, 16), -float(P), r(R_P, 16), ALU.mult, ALU.add))
            lane_row = kt[:, C_LANE:C_LANE + P].unsqueeze(1)
            def lanes_of(i):
                dve.tensor_tensor(lanes[:, 8 * i:8 * i + 8, :], bc(lane_row, 1, 8), spread(r(R_P + 8 * i, 8), P), ALU.is_equal).then_inc(lane_ok, 1)

            lanes_of(0)
            link(dve.tensor_tensor(r(R_T, NE, 7), spread(pos[:, 256:288], 7), bc(step.unsqueeze(1), 1, NE), ALU.is_gt))
            link(dve.tensor_reduce(r(R_OB, NE), r(R_T, NE, 7), AX.X, ALU.add))
            link(dve.tensor_tensor_scan(r(R_OC, NE), r(R_OB, NE), r(R_OB, NE), 0.0, ALU.add, ALU.bypass))
            link(dve.scalar_tensor_tensor(r(R_OX, NE), r(R_OC, NE), float(NE - 1), r(R_OB, NE), ALU.add, ALU.subtract))
            link(dve.tensor_tensor(r(R_OX, NE), r(R_OX, NE), iota[:, 0:NE], ALU.subtract))
            link(dve.tensor_tensor(r(R_T, 16, NE), r(R_O, 16, NE), bc(r(R_OX, NE).unsqueeze(1), 1, 16), ALU.mult))
            link(dve.tensor_reduce(r(R_OS, 16), r(R_T, 16, NE), AX.X, ALU.add))
            link(dve.tensor_tensor(r(R_OS, 16), r(R_OS, 16), r(R_B, 16), ALU.add))
            link(dve.scalar_tensor_tensor(r(R_OS, 16), r(R_B, 16), 1.0, r(R_OS, 16), ALU.is_ge, ALU.mult))
            link(dve.tensor_tensor(r(R_OS, 16), r(R_OS, 16), r(R_ID, 16), ALU.add))
            for i in range(2):
                of = slice(8 * i, 8 * i + 8)
                if i == 1:
                    lanes_of(1)
                link(dve.tensor_tensor(blocks[:, of, :], bc(iota.unsqueeze(1), 1, 8), spread(r(R_OS + 8 * i, 8), MAXB), ALU.is_equal))
                dve.tensor_tensor(recs[:, of, 0:MAXB], blocks[:, of, :], spread(kt[:, C_TOK + 8 * i:C_TOK + 8 * i + 8], MAXB), ALU.mult)
                link(dve.tensor_tensor(recs[:, of, MAXB:2 * MAXB], blocks[:, of, :], spread(r(R_W + 8 * i, 8), MAXB), ALU.mult))
                dve.sem_inc(rec_ok, 1)
            extra = MAXB - NE
            link(dve.tensor_tensor(r(R_T, extra, NE), spread(iota[:, 0:extra], NE), bc(r(R_OC, NE).unsqueeze(1), 1, extra), ALU.is_ge))
            link(dve.tensor_reduce(r(R_BT + NE, extra), r(R_T, extra, NE), AX.X, ALU.add))
            link(dve.tensor_scalar(r(R_BT + NE, extra), r(R_BT + NE, extra), float(NE - 1), None, ALU.min))
            link(dve.tensor_copy(r(R_BT, NE), iota[:, 0:NE]))
            link(dve.tensor_tensor(r(R_T, 8), bc(r(R_OC + NE - 1, 1), 1, 8), kt[:, C_ODD:C_ODD + 8], ALU.is_ge))
            link(dve.tensor_reduce(r(R_BT + MAXB, 1), r(R_T, 8), AX.X, ALU.add))
            link(dve.tensor_scalar(r(R_BT + MAXB, 1), r(R_BT + MAXB, 1), float(NE // 2 - 2), None, ALU.add))
            link(dve.tensor_copy(btab[:, 0:MAXB + 1], r(R_BT, MAXB + 1)))
            dve.sem_inc(np_ok, 1)
            dve.wait_ge(tab_mm, 1)
            dve.tensor_copy(tab[:, :, 2].bitcast(F32), ps[:, 7, MAXB:2 * MAXB])
            link(dve.tensor_scalar(r(R_T, MAXB), ps[:, 7, 0:MAXB], MISS, None, ALU.add))
            link(dve.tensor_scalar(r(R_T + 2 * MAXB, MAXB), r(R_T, MAXB), float(S), -float(S), ALU.is_ge, ALU.mult))
            dve.tensor_copy(tab[:, :, 1], r(R_T, MAXB))
            link(dve.tensor_tensor(tab[:, :, 0], r(R_T + 2 * MAXB, MAXB), r(R_T, MAXB), ALU.add))
            dve.sem_inc(tab_in, 1)

            n_pairs = dve.value_load(btab[0:1, MAXB:MAXB + 1], min_val=NE // 2 - 2, max_val=MAXB // 2 - 2) + 2

            def x_T(u, b):
                dve.wait_ge(xgT_mm, b + 1)
                dve.wait_ge(gu_mm, b - 1 if not isinstance(b, int) or b > 1 else 0)
                dve.tensor_copy(xgT[u][:, 0:4, :].rearrange("p k n -> p (k n)"), ps[:, 2, :]).then_inc(xgT_a, 1)

            def hidden(u, b):
                dve.wait_ge(sg_ok, b + 1)
                dve.wait_ge(hidT_mm, b - 1 if not isinstance(b, int) or b > 1 else 0)
                dve.tensor_tensor(hid[u][:, :], ps[:, u, FF:2 * FF], sg[u][:, :], ALU.mult).then_inc(hid_ok, 1)

            def hid_T(u, b, used):
                dve.wait_ge(hidT_mm, b + 1)
                dve.wait_ge(dn_mm, used)
                dve.tensor_copy(hidT[u][:, :, :].rearrange("p k n -> p (k n)"), ps[:, 4, 0:FF]).then_inc(hidT_ok, 1)

            def gated(u, b, stored):
                dve.wait_ge(dn_mm, b + 1)
                dve.wait_ge(y_put[u], stored)
                dve.tensor_scalar(yg[u][:, 512:D], ps[:, 6, :], tab[:, ds(b, 1), 2:3].bitcast(F32).rearrange("p a c -> p (a c)"), None, ALU.mult).then_inc(yg_b, 1)

            for i in range(2):
                dve.wait_ge(h2_saved[i], 64)
            dve.wait_ge(tab_in, 1)
            x_T(0, 0)
            hidden(0, 0)
            x_T(1, 1)
            with dve.Fori(1, n_pairs) as j:
                for u in (1, 0):
                    b = 2 * j - u
                    hid_T(1 - u, b - 1, 2 * j - 2)
                    x_T(1 - u, b + 1)
                    hidden(u, b)
                    gated(1 - u, b - 1, 16 * j - 16)
            last = 2 * n_pairs - 1
            hid_T(0, last - 1, last - 1)
            hidden(1, last)
            gated(0, last - 1, 16 * n_pairs - 16)
            hid_T(1, last, last - 1)
            gated(1, last, 16 * n_pairs - 16)

            def y_add(t):
                dve.wait_ge(y_in[t], 16)
                dve.tensor_tensor(yab[:, t, 0, :], yab[:, t, 0, :], yab[:, t, 1, :], ALU.add).then_inc(y_sum[0], 1)

            y_add(0)
            for t in range(T):
                y, o = yab[:, t, 0, :], yab[:, t, 1, :]
                if t % 2 == 1 and t + 1 < T:
                    y_add(t + 1)
                dve.wait_ge(y_root, t + 1)
                link(dve.reciprocal(fst[:, 16 + t:17 + t], fst[:, 8 + t:9 + t]))
                link(dve.scalar_tensor_tensor(o, y, fst[:, 16 + t:17 + t], mods[:, 3, :], ALU.mult, ALU.mult))
                dve.tensor_tensor(o, o, x1[:, t, :], ALU.add).then_inc(yo_ok, 1)

        @block.gpsimd
        def _(pool):
            def stage(kind, t, q_at, k_at):
                cols = slice(P * t, P * t + P)
                if kind == "k":
                    dst, src = ks[:, cols], kall[:, k_at, cols]
                else:
                    dst, src = qz[:, kind, cols], qall[:, q_at, cols]
                src = src.rearrange("p a n -> p (a n)") if len(src.shape) == 3 else src
                if kind == "k":
                    pool.tensor_copy(dst, src).then_inc(staged, 1)
                else:
                    pool.tensor_tensor(dst, src, bc(kt[:, C_HEAD + kind:C_HEAD + kind + 1], 1, P), ALU.mult).then_inc(staged, 1)

            def win_rest(n):
                pool.wait_ge(win_hi, n + 1)
                pool.tensor_tensor(wl[n % 2][:, :, :], wf[n % 2][:, :, :], wh[n % 2][:, :, :].bitcast(F32), ALU.subtract).then_inc(win_lo, 1)

            win_rest(0)
            pool.wait_ge(xr_ok, 2)
            for t in range(4, 6):
                pool.tensor_tensor(xs[:, t, :], xs[:, t, :], bc(xrs[:, t:t + 1], 1, D), ALU.mult).then_inc(x_pool, 1)
            flat = bias_b[:, :, :, :].rearrange("p m h c -> p m (h c)")
            pool.wait_ge(bias_ev, 16)
            for dst, src, mask in ((14, 2, C_RQ1), (15, 10, C_RQ0)):
                pool.tensor_tensor(flat[:, dst, :], flat[:, src, :], bc(kt[:, mask:mask + 1], 1, flat.shape[-1]), ALU.add).then_inc(bias_spec, 1)
            win_rest(1)

            pool.wait_ge(swT_ev, 12)
            pool.wait_ge(win_lo, 9)
            for kind, t, _ in STAGE_SW:
                stage(kind, t, 0, 0)
            with pool.Fori(0, 4) as hp:
                for kind, t, a in STAGE_SW:
                    pool.wait_ge(qk_mm, 16 * hp + (2 * a + 2))
                    pool.sem_inc(stage_due, 1)
                    stage(kind, t, ds(hp + 1, 1), ds((hp + 1) // 2, 1))
            with pool.Fori(0, 3) as hp:
                for kind, t, a in STAGE_NA:
                    pool.wait_ge(qk_mm, 16 * hp + (64 + 2 * a + 2))
                    pool.sem_inc(stage_due, 1)
                    stage(kind, t, ds(hp + 5, 1), ds(hp + 3, 1))
            pool.wait_ge(staged, 8 * STEPS)
            for n in range(4):
                pool.wait_ge(wout_in[n], 16)
                pool.tensor_copy(woh[n][:, :, :], wof[n][:, :, :]).then_inc(wout_hi, 1)
                pool.wait_ge(wout_hi, n + 1)
                pool.tensor_tensor(wol[n][:, :, :], wof[n][:, :, :], woh[n][:, :, :].bitcast(F32), ALU.subtract).then_inc(wout_lo, 1)
            pool.wait_ge(np_ok, 1)
            n_pairs = pool.value_load(btab[0:1, MAXB:MAXB + 1], min_val=NE // 2 - 2, max_val=MAXB // 2 - 2) + 2
            pool.wait_ge(tab_in, 1)
            for i in range(2):
                pool.wait_ge(h2_saved[i], 64)

            def index_in(dst, b, col, count):
                pool.tensor_copy(dst[:, :], tab[:, ds(b, 1), col:col + 1].rearrange("p a c -> p (a c)")).then_inc(ix_ok, 1)
                pool.wait_ge(ix_ok, count)
                pool.sem_inc(ix_due, 1)

            def fetch(u):
                pool.indirect_dma_start(xg[u][:, :], None, h2_dram, bass.IndirectOffsetOnAxis(ap=ixg[u][:, 0:1], axis=0),
                                        bounds_check=S - 1, oob_is_err=False).then_inc(xg_in[u], 16)

            def store(u, b, count):
                pool.wait_ge(yg_a, b + 1)
                pool.wait_ge(yg_b, b + 1)
                index_in(ixs[u], b, 1, count)
                pool.indirect_dma_start(y2_dram, bass.IndirectOffsetOnAxis(ap=ixs[u][:, 0:1], axis=0), yg[u][:, :], None,
                                        bounds_check=2 * S - 1, oob_is_err=False).then_inc(y_put[u], 16)

            def gather(u, b, count):
                index_in(ixg[u], b, 0, count)
                fetch(u)

            for b in range(4):
                if b >= 2:
                    pool.wait_ge(xgT_mm, b - 1)
                    pool.wait_ge(xg_in[b % 2], 16)
                gather(b % 2, b, b + 1)
            with pool.Fori(1, n_pairs - 1) as j:
                for u in (1, 0):
                    b = 2 * j - u
                    pool.wait_ge(xgT_mm, b + 2)
                    pool.wait_ge(xg_in[1 - u], 16 * j + 16)
                    gather(1 - u, b + 3, 4 * j + (3 - 2 * u))
                    store(1 - u, b - 1, 4 * j + (4 - 2 * u))
            for i in range(4):
                store(i % 2, 2 * n_pairs - 4 + i, 4 * n_pairs - 3 + i)
            for u in range(2):
                pool.wait_ge(y_put[u], 16 * n_pairs)
            pool.sem_inc(moe_done, 1)
            for t in range(1, T, 2):
                pool.wait_ge(y_in[t], 16)
                pool.tensor_tensor(yab[:, t, 0, :], yab[:, t, 0, :], yab[:, t, 1, :], ALU.add).then_inc(y_sum[1], 1)


def constants():
    c = np.zeros((P, C_END), np.float32)
    c[:, C_ID:C_ID + P] = np.eye(P)
    c[:, C_ONE:C_ONE + P] = 1
    c[:, C_TRI:C_TRI + P] = np.triu(np.ones((P, P)), 1)
    inv = np.float32(10000.0) ** (-np.arange(HD // 2, dtype=np.float32) * np.float32(2.0) / np.float32(HD))
    ang = np.arange(S, dtype=np.float32)[:, None] * inv[None, :].astype(np.float32)
    cos, sin = np.cos(ang).astype(np.float32), np.sin(ang).astype(np.float32)
    lay = lambda a: a.reshape(T, P, HD).transpose(1, 0, 2).reshape(P, T * HD)
    c[:, C_COS:C_COS + T * HD] = lay(np.concatenate([cos, cos], 1))
    c[:, C_SIN:C_SIN + T * HD] = lay(np.concatenate([-sin, sin], 1))
    q, key = np.arange(P)[:, None], np.arange(3 * P)[None, :] - P
    c[:, C_SWM:C_SWM + 3 * P] = np.where(np.abs(key - q) <= P, 0, NEG)
    col, kc = (np.arange(P) % GRID_W)[:, None], np.arange(GRID_W)[None, :]
    start = np.clip(col - KW // 2, 0, GRID_W - KW)
    c[:, C_NAM:C_NAM + GRID_W] = np.where((kc >= start) & (kc < start + KW), 0, NEG)
    for r in range(2):
        for dc in range(2 * KW - 1):
            c[32 * r + dc, C_SEL + 64 * r + 78 - dc] = 1
    c[:, C_IOTA:C_IOTA + MAXB] = np.arange(MAXB)
    c[:, C_STEP:C_STEP + 8] = P * (1 + np.arange(8))
    c[:, C_ODD:C_ODD + 8] = 1 + 2 * np.arange(8)
    tok = np.arange(P)[:, None] + P * np.arange(T)[None, :]
    c[:, C_TOK:C_TOK + 16] = np.concatenate([tok, tok + S], 1) - MISS
    c[:, C_LANE:C_LANE + P] = np.arange(P)
    c[:, C_RQ0], c[:, C_RQ1] = np.where(np.arange(P) < 64, NEG, 0), np.where(np.arange(P) < 64, 0, NEG)
    c[:, C_EPS] = EPS
    c[:64, C_HEAD], c[64:, C_HEAD + 1] = 1, 1
    c[:, C_PLUS:C_PLUS + 2] = 1
    return c


def kernel(**a):
    import concourse.bacc as bacc
    from concourse.bass_utils import run_bass_kernel_spmd

    a = {k: np.asarray(v) for k, v in a.items()}
    cols = lambda v: v.reshape(-1, P).T

    def chunks(w, order):
        n = w.shape[1] // CH
        return np.ascontiguousarray(w.reshape(K, P, n, CH).transpose(2, 1, 0, 3)[order])

    b = a["b_ada"][0]
    rpb = a["na_rpb"][0]
    rcols = np.zeros((63, 14, 8), np.float32)
    for r in range(2):
        rcols[32 * r:32 * r + 31] = rpb[:, 1 - r:15 - r, :].transpose(2, 1, 0)
    wr = np.concatenate([a["w_group_router"][0]] + [a["w_expert_router"][0, g] for g in range(NG)], 1)
    gu = np.concatenate([a["w_gate"][0], a["w_up"][0]], 2)
    arrays = {
        "x": a["x"][0],
        "consts": constants(),
        "vecs": np.concatenate([cols(b[:2 * D]), cols(a["g_pre_mix"][0]), cols(a["c"][0])], 1),
        "b_rows": b[2 * D:].reshape(8, 512),
        "g_rows": np.stack([a["g_post_mix"][0], a["g_pre_ffn"][0], a["g_post_ffn"][0],
                            np.concatenate([a["beta_na"][0], a["beta_swa"][0]])]),
        "rpb_cols": rcols.reshape(63, 112),
        "sinks": a["swa_sinks"],
        "w_mix_ada": a["w_ada"][0, :, :2 * D].reshape(K, P, 4, 512).transpose(2, 1, 0, 3),
        "w_ada": chunks(a["w_ada"][0], np.arange(8, 24)),
        "w_in": chunks(a["w_in"][0], np.array([8, 6, 7, 4, 5, 0, 1, 2, 3])),
        "w_out": chunks(a["w_out"][0], np.arange(4)),
        "w_router": wr.reshape(K, P, 36).transpose(1, 0, 2),
        "w_gu": gu.reshape(NE, K, P, 2 * FF).transpose(0, 2, 1, 3),
        "w_down": a["w_down"][0].reshape(NE, 2, P, D).transpose(0, 2, 1, 3),
    }
    arrays = {f"in_{k}": np.ascontiguousarray(v) for k, v in arrays.items()}
    nc = bacc.Bacc("TRN2", target_bir_lowering=False, num_devices=1)
    aps = [nc.dram_tensor(k, v.shape, mybir.dt.from_np(v.dtype), kind="ExternalInput").ap() for k, v in arrays.items()]
    out = nc.dram_tensor("out_dram", (S, D), F32, kind="ExternalOutput").ap()
    build(nc, *aps, out)
    r = run_bass_kernel_spmd(nc, [arrays], core_ids=[0])
    return r.results[0]["out_dram"].reshape(1, S, D)
```
